# Optimizing a Trainium2 kernel written in Bass

```python
import math
import jax, jax.numpy as jnp
from jax import lax
import numpy as np

D_MODEL = 1024
BATCH = 1
SEQ = 256
DEPTH = 1

HG_HEADS = 4
HG_KDIM = 128
HG_VDIM = 128
HG_WIDTH = HG_HEADS * HG_KDIM
CHUNK = 32
LRU_WIDTH = 512
LRU_BLOCKS = 8
LRU_BLOCK_DIM = LRU_WIDTH // LRU_BLOCKS
CONV_WIDTH = 4
LRU_C = 8.0
D_MIX = HG_WIDTH + LRU_WIDTH
D_IN = 4 * HG_WIDTH + 2 * LRU_WIDTH
D_FF = -(-8 * D_MODEL // (3 * 256)) * 256
EPS = 1e-6


def rms_norm(x, w):
    xf = x.astype(jnp.float32)
    y = xf * lax.rsqrt(jnp.mean(xf * xf, axis=-1, keepdims=True) + EPS)
    return (y * w.astype(jnp.float32)).astype(x.dtype)

def hgrn2_mix(q, f_logit, i, g, lb, norm_w):
    B, S, _ = q.shape
    out_dtype = q.dtype
    qf = jax.nn.silu(q.astype(jnp.float32))
    f = lb + (1.0 - lb) * jax.nn.sigmoid(f_logit.astype(jnp.float32))
    log_f = jnp.log(f)
    k = 1.0 - f
    v = i.astype(jnp.float32)
    n_chunks = S // CHUNK

    def to_chunks(t, d):
        return t.reshape(B, n_chunks, CHUNK, HG_HEADS, d).transpose(1, 0, 3, 2, 4)

    qc, kc, gc, vc = to_chunks(qf, HG_KDIM), to_chunks(k, HG_KDIM), to_chunks(log_f, HG_KDIM), to_chunks(v, HG_VDIM)
    causal = jnp.tril(jnp.ones((CHUNK, CHUNK), dtype=bool))

    def step(state, xs):
        q_, k_, lg, v_ = xs
        b = jnp.cumsum(lg, axis=-2)
        b_last = b[..., -1:, :]
        q_dec = q_ * jnp.exp(b)
        k_dec = k_ * jnp.exp(-b)
        scores = jnp.where(causal, jnp.einsum('bhtk,bhsk->bhts', q_dec, k_dec), 0.0)
        o = jnp.einsum('bhts,bhsv->bhtv', scores, v_) + jnp.einsum('bhtk,bhkv->bhtv', q_dec, state)
        k_state = k_ * jnp.exp(b_last - b)
        new_state = jnp.exp(b_last)[..., 0, :, None] * state + jnp.einsum('bhsk,bhsv->bhkv', k_state, v_)
        return new_state, o

    state0 = jnp.zeros((B, HG_HEADS, HG_KDIM, HG_VDIM), jnp.float32)
    _, o = lax.scan(step, state0, (qc, kc, gc, vc))
    o = o.transpose(1, 0, 3, 2, 4).reshape(B, S, HG_HEADS, HG_VDIM)
    o = o * lax.rsqrt(jnp.mean(o * o, axis=-1, keepdims=True) + EPS) * norm_w.astype(jnp.float32)
    o = o * jax.nn.silu(g.astype(jnp.float32).reshape(B, S, HG_HEADS, HG_VDIM))
    return o.reshape(B, S, HG_WIDTH).astype(out_dtype)

def rglru_mix(xb, gate_b, conv_w, conv_b, wa, ba, wx, bx, a_param):
    B, S, W = xb.shape
    out_dtype = xb.dtype
    x_pad = jnp.pad(xb, ((0, 0), (CONV_WIDTH - 1, 0), (0, 0)))
    xc = conv_b + sum(x_pad[:, tap:tap + S] * conv_w[tap] for tap in range(CONV_WIDTH))
    xc = xc.astype(jnp.float32)
    xblk = xc.reshape(B, S, LRU_BLOCKS, LRU_BLOCK_DIM)
    r = jax.nn.sigmoid(jnp.einsum('bsnd,nde->bsne', xblk, wa.astype(jnp.float32)).reshape(B, S, W) + ba)
    ig = jax.nn.sigmoid(jnp.einsum('bsnd,nde->bsne', xblk, wx.astype(jnp.float32)).reshape(B, S, W) + bx)
    log_a = -LRU_C * r * jax.nn.softplus(-a_param.astype(jnp.float32))
    a = jnp.exp(log_a)
    b_in = jnp.sqrt(-jnp.expm1(2.0 * log_a)) * (ig * xc)

    def combine(lhs, rhs):
        a1, b1 = lhs
        a2, b2 = rhs
        return a1 * a2, a2 * b1 + b2

    _, h = lax.associative_scan(combine, (a, b_in), axis=1)
    y = h * jax.nn.gelu(gate_b.astype(jnp.float32), approximate=True)
    return y.astype(out_dtype)

def first_inputs(seed: int = 0) -> dict:
    key = jax.random.key(seed)
    ks = jax.random.split(key, 20)
    f32 = jnp.float32
    nrm = lambda k, shape, scale: (jax.random.normal(k, shape, f32) * scale)
    s_lru = jax.random.uniform(ks[12], (DEPTH, LRU_WIDTH), f32, 0.9, 0.999) ** (1.0 / LRU_C)
    return {
        'x': nrm(ks[0], (BATCH, SEQ, D_MODEL), 1.0),
        'mix_norm_w': 1.0 + nrm(ks[1], (DEPTH, D_MODEL), 0.02),
        'w_in': nrm(ks[2], (DEPTH, D_MODEL, D_IN), D_MODEL ** -0.5),
        'hg_lb': nrm(ks[3], (DEPTH + 1, HG_WIDTH), 0.5),
        'hg_norm_w': 1.0 + nrm(ks[4], (DEPTH, HG_VDIM), 0.02),
        'conv_w': nrm(ks[5], (DEPTH, CONV_WIDTH, LRU_WIDTH), CONV_WIDTH ** -0.5),
        'conv_b': nrm(ks[6], (DEPTH, LRU_WIDTH), 0.02),
        'lru_wa': nrm(ks[7], (DEPTH, LRU_BLOCKS, LRU_BLOCK_DIM, LRU_BLOCK_DIM), LRU_BLOCK_DIM ** -0.5),
        'lru_ba': nrm(ks[8], (DEPTH, LRU_WIDTH), 0.02),
        'lru_wx': nrm(ks[9], (DEPTH, LRU_BLOCKS, LRU_BLOCK_DIM, LRU_BLOCK_DIM), LRU_BLOCK_DIM ** -0.5),
        'lru_bx': nrm(ks[10], (DEPTH, LRU_WIDTH), 0.02),
        'lru_a': jnp.log(s_lru) - jnp.log1p(-s_lru),
        'w_out': nrm(ks[11], (DEPTH, D_MIX, D_MODEL), D_MIX ** -0.5),
        'ffn_norm_w': 1.0 + nrm(ks[13], (DEPTH, D_MODEL), 0.02),
        'w_gate_up': nrm(ks[14], (DEPTH, D_MODEL, 2 * D_FF), D_MODEL ** -0.5),
        'w_down': nrm(ks[15], (DEPTH, D_FF, D_MODEL), D_FF ** -0.5),
        'final_norm_w': 1.0 + nrm(ks[16], (D_MODEL,), 0.02),
    }

def first_block(x, mix_norm_w, w_in, hg_lb, hg_norm_w, conv_w, conv_b, lru_wa, lru_ba,
              lru_wx, lru_bx, lru_a, w_out, ffn_norm_w, w_gate_up, w_down, final_norm_w):
    lb_all = jnp.cumsum(jax.nn.softmax(hg_lb.astype(jnp.float32), axis=0), axis=0)
    h = x
    for l in range(DEPTH):
        xn = rms_norm(h, mix_norm_w[l])
        proj = jnp.einsum('bsd,de->bse', xn, w_in[l])
        q, f_logit, i_v, g, lru_x, lru_gate = jnp.split(
            proj, [HG_WIDTH, 2 * HG_WIDTH, 3 * HG_WIDTH, 4 * HG_WIDTH, 4 * HG_WIDTH + LRU_WIDTH], axis=-1)
        o_hg = hgrn2_mix(q, f_logit, i_v, g, lb_all[l], hg_norm_w[l])
        o_lru = rglru_mix(lru_x, lru_gate, conv_w[l], conv_b[l], lru_wa[l], lru_ba[l],
                          lru_wx[l], lru_bx[l], lru_a[l])
        mixed = jnp.concatenate([o_hg, o_lru], axis=-1)
        h = h + jnp.einsum('bse,ed->bsd', mixed, w_out[l])
        hn = rms_norm(h, ffn_norm_w[l])
        gate, up = jnp.split(jnp.einsum('bsd,df->bsf', hn, w_gate_up[l]), 2, axis=-1)
        h = h + jnp.einsum('bsf,fd->bsd', jax.nn.silu(gate) * up, w_down[l])
    return rms_norm(h, final_norm_w)


D_MIX_2 = D_MODEL
HEAD_DIM = 64
RET_WIDTH = D_MIX_2 // 2
SB_WIDTH = D_MIX_2 - RET_WIDTH
N_RET_HEADS = RET_WIDTH // HEAD_DIM
N_SB_HEADS = SB_WIDTH // HEAD_DIM
RET_CHUNK = 128
SB_BLOCK = 128
ROPE_BASE = 10000.0
IN_COLS = 4 * RET_WIDTH + 3 * SB_WIDTH
N_KEYS = 128
N_EXPERTS = N_KEYS * N_KEYS
PEER_HEADS = 8
PEER_TOPK = 16
PEER_QDIM = 256
PEER_HALF = PEER_QDIM // 2
PEER_BLOCK = 128


def rms_norm_2(x, gain):
    xf = x.astype(jnp.float32)
    y = xf * lax.rsqrt(jnp.mean(xf * xf, axis=-1, keepdims=True) + EPS)
    return (y * gain.astype(jnp.float32)).astype(x.dtype)

def rotary(x, positions):
    half = HEAD_DIM // 2
    inv_freq = ROPE_BASE ** (-jnp.arange(half, dtype=jnp.float32) / half)
    ang = positions.astype(jnp.float32)[..., None] * inv_freq
    cos = jnp.cos(ang)[:, :, None, :]
    sin = jnp.sin(ang)[:, :, None, :]
    x1 = x[..., :half].astype(jnp.float32)
    x2 = x[..., half:].astype(jnp.float32)
    out = jnp.concatenate([x1 * cos - x2 * sin, x2 * cos + x1 * sin], axis=-1)
    return out.astype(x.dtype)

def retention(q, k, v, positions):
    B, S, H, D = q.shape
    C = RET_CHUNK
    NC = S // C
    q = rotary(q, positions)
    k = rotary(k, positions) * (D ** -0.5)
    log_g = jnp.log1p(-(2.0 ** (-5.0 - jnp.arange(H, dtype=jnp.float32))))
    idx = jnp.arange(C, dtype=jnp.float32)
    rel = idx[:, None] - idx[None, :]
    decay_intra = jnp.where(rel >= 0, jnp.exp(log_g[:, None, None] * jnp.maximum(rel, 0.0)), 0.0)
    xi = jnp.exp(log_g[:, None] * (idx + 1.0))
    zeta = jnp.exp(log_g[:, None] * (C - 1.0 - idx))
    chunk_decay = jnp.exp(log_g * C)
    qc = q.reshape(B, NC, C, H, D)
    kc = k.reshape(B, NC, C, H, D)
    vc = v.reshape(B, NC, C, H, D)
    scores = jnp.einsum('bnihd,bnjhd->bnhij', qc, kc) * decay_intra
    y_intra = jnp.einsum('bnhij,bnjhd->bnihd', scores, vc)
    kv = jnp.einsum('bnjhd,hj,bnjhe->nbhde', kc, zeta, vc).astype(jnp.float32)

    def step(state, kv_i):
        return chunk_decay[None, :, None, None] * state + kv_i, state

    _, states = lax.scan(step, jnp.zeros((B, H, D, D), jnp.float32), kv)
    y_cross = jnp.einsum('bnihd,nbhde,hi->bnihe', qc, states, xi)
    return (y_intra + y_cross).reshape(B, S, H, D)

def head_group_norm(y, gain):
    B, S, H, D = y.shape
    yf = y.astype(jnp.float32)
    mu = jnp.mean(yf, axis=-1, keepdims=True)
    var = jnp.mean(jnp.square(yf - mu), axis=-1, keepdims=True)
    yn = (yf - mu) * lax.rsqrt(var + EPS)
    return yn.reshape(B, S, H * D) * gain.astype(jnp.float32)

def stick_breaking(q, k, v):
    B, S, H, D = q.shape
    NB = S // SB_BLOCK
    q_blocks = q.reshape(B, NB, SB_BLOCK, H, D).transpose(1, 0, 3, 2, 4)
    kt = k.transpose(0, 2, 1, 3)
    vt = v.transpose(0, 2, 1, 3)
    key_pos = jnp.arange(S)
    scale = D ** -0.5

    def block(args):
        qi, start = args
        z = jnp.einsum('bhqd,bhsd->bhqs', qi, kt).astype(jnp.float32) * scale
        q_pos = start + jnp.arange(SB_BLOCK)
        mask = key_pos[None, :] < q_pos[:, None]
        log_beta = jax.nn.log_sigmoid(z)
        log_stay = jnp.where(mask, log_beta - z, 0.0)
        log_w = log_beta + lax.cumsum(log_stay, axis=3, reverse=True) - log_stay
        w = jnp.where(mask, jnp.exp(log_w), 0.0)
        return jnp.einsum('bhqs,bhsd->bhqd', w.astype(vt.dtype), vt)

    starts = jnp.arange(NB) * SB_BLOCK
    out = lax.map(block, (q_blocks, starts))
    return out.transpose(1, 0, 3, 2, 4).reshape(B, S, H, D)

def peer(h, w_query, sub_keys, expert_down, expert_up):
    B, S, Dm = h.shape
    T = B * S
    K = PEER_TOPK
    ht = h.reshape(T, Dm)
    qry = (ht @ w_query).reshape(T, PEER_HEADS, 2, PEER_HALF)
    sub_scores = jnp.einsum('thpc,hpkc->thpk', qry, sub_keys).astype(jnp.float32)
    top_s, top_i = lax.top_k(sub_scores, K)
    cand_s = top_s[:, :, 0, :, None] + top_s[:, :, 1, None, :]
    cand_id = top_i[:, :, 0, :, None] * N_KEYS + top_i[:, :, 1, None, :]
    best_s, best_c = lax.top_k(cand_s.reshape(T, PEER_HEADS, K * K), K)
    expert_id = jnp.take_along_axis(cand_id.reshape(T, PEER_HEADS, K * K), best_c, axis=-1)
    gate = jax.nn.softmax(best_s, axis=-1)
    NBK = T // PEER_BLOCK
    ids = expert_id.reshape(NBK, PEER_BLOCK, PEER_HEADS * K)
    gates = gate.reshape(NBK, PEER_BLOCK, PEER_HEADS * K)
    xs = ht.reshape(NBK, PEER_BLOCK, Dm)

    def block(args):
        xb, ib, gb = args
        u = expert_down[ib]
        a = jnp.einsum('pd,ped->pe', xb, u).astype(jnp.float32)
        act = jax.nn.gelu(a, approximate=False) * gb
        v = expert_up[ib]
        return jnp.einsum('pe,ped->pd', act.astype(xb.dtype), v)

    y = lax.map(block, (xs, ids, gates))
    return y.reshape(B, S, Dm)

def second_inputs(seed: int = 0) -> dict:
    key = jax.random.key(seed)
    ks = jax.random.split(key, 16)
    f32 = jnp.float32
    nrm = lambda k, shape, s: jax.random.normal(k, shape, f32) * s
    return {
        "x": nrm(ks[0], (BATCH, SEQ, D_MODEL), 1.0),
        "c": nrm(ks[1], (BATCH, D_MODEL), 1.0),
        "positions": jnp.broadcast_to(jnp.arange(SEQ, dtype=jnp.int32)[None, :], (BATCH, SEQ)),
        "ada_w": nrm(ks[2], (DEPTH, D_MODEL, 6 * D_MODEL), D_MODEL ** -0.5),
        "ada_b": nrm(ks[3], (DEPTH, 6 * D_MODEL), 0.1),
        "norm1_gain": 1.0 + nrm(ks[4], (DEPTH, D_MODEL), 0.1),
        "norm2_gain": 1.0 + nrm(ks[5], (DEPTH, D_MODEL), 0.1),
        "w_in": nrm(ks[6], (DEPTH, D_MODEL, IN_COLS), D_MODEL ** -0.5),
        "ret_norm_gain": 1.0 + nrm(ks[7], (DEPTH, RET_WIDTH), 0.1),
        "sb_q_gain": 1.0 + nrm(ks[8], (DEPTH, HEAD_DIM), 0.1),
        "sb_k_gain": 1.0 + nrm(ks[9], (DEPTH, HEAD_DIM), 0.1),
        "sb_out_gain": 1.0 + nrm(ks[10], (DEPTH, HEAD_DIM), 0.1),
        "w_out": nrm(ks[11], (DEPTH, D_MIX_2, D_MODEL), D_MIX_2 ** -0.5),
        "peer_w_query": nrm(ks[12], (DEPTH, D_MODEL, PEER_HEADS * PEER_QDIM), D_MODEL ** -0.5),
        "peer_sub_keys": nrm(ks[13], (DEPTH, PEER_HEADS, 2, N_KEYS, PEER_HALF), PEER_HALF ** -0.5),
        "peer_down": nrm(ks[14], (DEPTH, N_EXPERTS, D_MODEL), D_MODEL ** -0.5),
        "peer_up": nrm(ks[15], (DEPTH, N_EXPERTS, D_MODEL), PEER_HEADS ** -0.5),
    }

def second_block(x, c, positions, ada_w, ada_b, norm1_gain, norm2_gain, w_in, ret_norm_gain,
              sb_q_gain, sb_k_gain, sb_out_gain, w_out, peer_w_query, peer_sub_keys,
              peer_down, peer_up):
    B, S, _ = x.shape
    for layer in range(DEPTH):
        mod = jax.nn.silu(c) @ ada_w[layer] + ada_b[layer]
        shift1, scale1, gate1, shift2, scale2, gate2 = jnp.split(mod[:, None, :], 6, axis=-1)

        h = rms_norm_2(x, norm1_gain[layer]) * (1.0 + scale1) + shift1
        proj = h @ w_in[layer]
        r_q, r_k, r_v, r_g, s_q, s_k, s_v = jnp.split(
            proj, np.cumsum([RET_WIDTH] * 4 + [SB_WIDTH] * 2), axis=-1)
        heads_r = lambda t: t.reshape(B, S, N_RET_HEADS, HEAD_DIM)
        heads_s = lambda t: t.reshape(B, S, N_SB_HEADS, HEAD_DIM)

        y_ret = retention(heads_r(r_q), heads_r(r_k), heads_r(r_v), positions)
        y_ret = head_group_norm(y_ret, ret_norm_gain[layer]) * jax.nn.silu(r_g.astype(jnp.float32))

        q_sb = rms_norm_2(heads_s(s_q), sb_q_gain[layer])
        k_sb = rms_norm_2(heads_s(s_k), sb_k_gain[layer])
        y_sb = stick_breaking(q_sb, k_sb, heads_s(s_v))
        y_sb = rms_norm_2(y_sb, sb_out_gain[layer]).reshape(B, S, SB_WIDTH)

        mixed = jnp.concatenate([y_ret.astype(x.dtype), y_sb.astype(x.dtype)], axis=-1) @ w_out[layer]
        x = x + gate1 * mixed

        h2 = rms_norm_2(x, norm2_gain[layer]) * (1.0 + scale2) + shift2
        ffn = peer(h2, peer_w_query[layer], peer_sub_keys[layer], peer_down[layer], peer_up[layer])
        x = x + gate2 * ffn
    return x


def setup_inputs(seed=0):
    out = dict(first_inputs(seed))
    for name, value in second_inputs(seed + 1).items():
        if name != "x":
            out[name + "_2"] = value
    return out


def reference(
    x, mix_norm_w, w_in, hg_lb, hg_norm_w, conv_w, conv_b, lru_wa, lru_ba, lru_wx, lru_bx,
    lru_a, w_out, ffn_norm_w, w_gate_up, w_down, final_norm_w, c_2, positions_2, ada_w_2,
    ada_b_2, norm1_gain_2, norm2_gain_2, w_in_2, ret_norm_gain_2, sb_q_gain_2, sb_k_gain_2,
    sb_out_gain_2, w_out_2, peer_w_query_2, peer_sub_keys_2, peer_down_2, peer_up_2,
):
    x = first_block(
        x, mix_norm_w, w_in, hg_lb, hg_norm_w, conv_w, conv_b, lru_wa, lru_ba, lru_wx, lru_bx,
        lru_a, w_out, ffn_norm_w, w_gate_up, w_down, final_norm_w,
    )
    return second_block(
        x, c_2, positions_2, ada_w_2, ada_b_2, norm1_gain_2, norm2_gain_2, w_in_2,
        ret_norm_gain_2, sb_q_gain_2, sb_k_gain_2, sb_out_gain_2, w_out_2, peer_w_query_2,
        peer_sub_keys_2, peer_down_2, peer_up_2,
    )


_drawn_inputs = setup_inputs


def setup_inputs(seed=0):
    import zlib

    import numpy as np

    out = dict(_drawn_inputs(seed))
    spreads = {}
    factors = {'hg_norm_w': 3.828,
     'lru_ba': 38.463,
     'lru_bx': 24.39,
     'sb_q_gain_2': 2.954,
     'sb_k_gain_2': 2.955,
     'ffn_norm_w': 3.146}
    for name, (base, spread) in spreads.items():
        noise = np.random.default_rng([zlib.crc32(name.encode()), seed]).standard_normal(out[name].shape)
        drawn = base * np.exp(spread * noise) if base else spread * noise
        out[name] = __import__('jax').numpy.asarray(drawn.astype(out[name].dtype))
    for name, factor in factors.items():
        out[name] = (out[name] * factor).astype(out[name].dtype)
    return out
```

```python
import math
from contextlib import ExitStack

import numpy as np

import concourse.bass as bass
from concourse import mybir

ALU = mybir.AluOpType
ACT = mybir.ActivationFunctionType
F32 = mybir.dt.float32
U32 = mybir.dt.uint32
I32 = mybir.dt.int32
AX_X = mybir.AxisListType.X

T = 256
D = 1024
KD = D // 128
FF = 2816
NF = FF // 128
CH = 32
NCH = T // CH
LRU_C = 8.0
EPS = 1e-6
SLOTS = 20
NEXP = 16384
NEG = -3.0e38

VEC = {}
_at = 0
for _name, _n in (("mix", 8), ("ffn", 8), ("fin", 8), ("n1", 8), ("n2", 8), ("conv", 16), ("convb", 4), ("ba", 4),
                  ("bx", 4), ("la", 4), ("lb0", 4), ("lb1", 4), ("hgn", 1), ("retg", 4), ("sbq", 1), ("sbk", 1),
                  ("sbo", 1), ("adab", 48), ("c", 8)):
    VEC[_name] = (_at, _n)
    _at += _n
NVEC = _at

CST = {}
_at = 0
for _name, _n in (("ident", 128), ("rot", 128), ("ones", 128), ("bd64", 128), ("tri", 128), ("sbm", 128),
                  ("hgm", 128), ("iota", 16), ("invf", 1), ("eps", 1), ("one", 1), ("zero", 1)):
    CST[_name] = (_at, _n)
    _at += _n
NCST = _at


def shape_constants():
    c = np.zeros((128, NCST), np.float32)

    def put(name, a):
        s, n = CST[name]
        c[:, s:s + n] = np.asarray(a, np.float32).reshape(128, n)

    p = np.arange(128)
    put("ident", np.eye(128))
    rot = np.zeros((128, 128))
    for m in range(128):
        if m % 64 < 32:
            rot[m + 32, m] = -1.0
        else:
            rot[m - 32, m] = 1.0
    put("rot", rot)
    put("ones", np.ones((128, 128)))
    put("bd64", (p[:, None] // 64 == p[None, :] // 64) / 64.0)
    put("tri", p[:, None] > p[None, :])
    put("sbm", p[:, None] < p[None, :])
    put("hgm", (p[:, None] // CH == p[None, :] // CH) & (p[:, None] <= p[None, :]))
    put("iota", np.tile(np.arange(16), (128, 1)))
    put("invf", np.float32(10000.0) ** (-(p % 32).astype(np.float32) / np.float32(32)))
    put("eps", np.full(128, EPS))
    put("one", np.ones(128))
    dec = np.zeros((128, 8, T), np.float32)
    rel = np.arange(T)[None, :] - p[:, None]
    for h in range(8):
        lg = np.float32(np.log1p(-(2.0 ** (-5.0 - h))))
        dec[:, h] = np.where(rel >= 0, np.exp(np.float64(lg) * np.maximum(rel, 0)) * 0.125, 0.0)
    return c, dec.reshape(128, 8 * T)


class Queue:

    def __init__(self, sem):
        self.sem, self.n, self.items, self.past = sem, 0, [], {}

    def wait(self, *tickets):
        for sem, v in tickets:
            if self.past.get(sem.num, 0) < v:
                self.past[sem.num] = v
                self.items.append(lambda e, sem=sem, v=v: e.wait_ge(sem, v))

    def quiet(self, fn, *tickets):
        self.wait(*tickets)
        self.items.append(fn)

    def do(self, fn, *tickets):
        self.wait(*tickets)
        self.n += 1
        self.items.append(lambda e: fn(e).then_inc(self.sem, 1))
        return self.sem, self.n

    def run(self, eng):
        for f in self.items:
            f(eng)


def build(nc, xT, vecs, cst, decay, pos, w_in, w_out, w_gu, w_down, ada, w_in2, w_out2, w_q, subk, lru_w,
          peer_down, peer_up, out):
    ctx = ExitStack()
    with ctx:
        def sb(name, n, dt=F32):
            return ctx.enter_context(nc.sbuf_tensor(name, [128, n], dt))

        def sem(name):
            return ctx.enter_context(nc.semaphore(name))

        ring_sb = sb("ring_sb", SLOTS * 1024)
        hT = sb("hT", 2048)
        xn = sb("xn", 2048)
        sq = sb("sq", 2048)
        cs = sb("cs", NCST)
        vv = sb("vv", NVEC)
        cosT = sb("cosT", T)
        sinT = sb("sinT", T)
        posi = sb("posi", T, I32)
        rstd = sb("rstd", 512)
        stdt = sb("stdt", 512)
        small = sb("small", 256)
        arena = sb("arena", 20 * 1024)
        pb = [ctx.enter_context(nc.psum_tensor(f"pb{i}", [128, 512], F32)) for i in range(8)]

        def blk(i, n=1024):
            return arena[:, i * 1024:i * 1024 + n]

        def v3(ap, m):
            return ap.rearrange("p (n m) -> p n m", m=m)

        def c_(name):
            s, n = CST[name]
            return cs[:, s:s + n]

        def vc(name, j=0, n=1):
            s = VEC[name][0] + j
            return vv[:, s:s + n]

        P = Queue(sem("s_pe"))
        V = Queue(sem("s_dve"))
        A = Queue(sem("s_act"))
        G = Queue(sem("s_pool"))
        SY = Queue(sem("s_sp"))
        s_ld = [sem(f"s_ld{i}") for i in range(3)]
        s_slot = [sem(f"s_slot{i}") for i in range(SLOTS)]
        s_row = [sem(f"s_row{i}") for i in range(SLOTS)]
        s_out = sem("s_out")

        def act(o, i, f, *t, **kw):
            return A.do(lambda e: e.activation(o, i, f, **kw), *t)

        def tt(o, a, b, op, *t):
            return V.do(lambda e: e.tensor_tensor(o, a, b, op), *t)

        def ts(o, a, s1, op0, *t, s2=None, op1=None):
            if op1 is None:
                return V.do(lambda e: e.tensor_scalar(o, a, s1, None, op0), *t)
            return V.do(lambda e: e.tensor_scalar(o, a, s1, s2, op0, op1), *t)

        def stt(o, a, s, b, op0, op1, *t):
            return V.do(lambda e: e.scalar_tensor_tensor(out=o, in0=a, scalar=s, in1=b, op0=op0, op1=op1), *t)

        def vcopy(o, i, *t):
            return V.do(lambda e: e.tensor_copy(o, i), *t)

        def recip(o, i, *t):
            return V.do(lambda e: e.reciprocal(o, i), *t)

        def mm(o, l, r, start, stop, *t, sig=False, skip=False):
            fn = lambda e: e.matmul(o, l, r, start=start, stop=stop, skip_group_check=skip)
            return P.do(fn, *t) if sig else P.quiet(fn, *t)

        MUL, ADD, SUB, MAX, MIN = ALU.mult, ALU.add, ALU.subtract, ALU.max, ALU.min

        readers = [[] for _ in range(8)]
        turn = [0]
        ringset = [[0, 1, 2, 3]]

        def bank(i=None):
            if i is None:
                i = ringset[0][turn[0] % len(ringset[0])]
                turn[0] += 1
            P.wait(*readers[i])
            readers[i] = []
            return i

        units, freed = [], {}

        def unit(src):
            units.append(src)
            return len(units) - 1

        def align():
            while len(units) % 4:
                unit(None)

        def slot(u):
            return ring_sb[:, (u % SLOTS) * 1024:(u % SLOTS + 1) * 1024]

        def landed(u):
            uses = sum(1 for x in range(u % SLOTS, u + 1, SLOTS) if units[x] is not None)
            return s_slot[u % SLOTS], 16 * uses

        def gemm(us, rhs, t=(), b=None, nk=KD):
            b = bank(b)
            for i, u in enumerate(us):
                P.wait(landed(u), *t)
                for k in range(nk):
                    w = slot(u)[:, k * 128:(k + 1) * 128]
                    if k < nk - 1:
                        mm(pb[b][:, i * 256:(i + 1) * 256], w, rhs(k), k == 0, False)
                    else:
                        tk = mm(pb[b][:, i * 256:(i + 1) * 256], w, rhs(k), False, True, sig=True)
                freed[u] = tk
            return b, tk

        def gemm_tok(us, lhs, tile, t=(), last=False):
            b = bank()
            for u in us:
                P.wait(landed(u))
            P.wait(*t)
            s0 = us[0] % SLOTS
            w = ring_sb[:, s0 * 1024:(s0 + 4) * 1024].rearrange("p (u k c) -> p k u c", u=4, c=128)
            for k in range(KD):
                tk = mm(pb[b][:, :], lhs(k)[:, tile * 128:(tile + 1) * 128], w[:, k], k == 0, k == KD - 1,
                        sig=k == KD - 1)
            if last:
                for u in us:
                    freed[u] = tk
            return b, tk

        SY.quiet(lambda e: e.dma_start(cs[:, :], cst).then_inc(s_ld[0], 16))
        SY.quiet(lambda e: e.dma_start(vv[:, :], vecs).then_inc(s_ld[0], 16))
        SY.quiet(lambda e: e.dma_start(hT[:, :], xT).then_inc(s_ld[1], 16))
        A.quiet(lambda e: e.dma_start(posi[:, :], pos.to_broadcast([128, T])).then_inc(s_ld[2], 16))
        L_cst, L_x, L_pos = (s_ld[0], 32), (s_ld[1], 16), (s_ld[2], 16)

        for q in (P, V, A):
            q.wait(L_cst)

        U_f = [unit(w_in[4 + i]) for i in range(4)]
        U_qq = [unit(w_in[i]) for i in range(4)]
        U_i = [unit(w_in[8 + i]) for i in range(4)]
        U_lx = [unit(w_in[16 + i]) for i in range(4)]
        U_lw = unit(lru_w)
        U_lg = [unit(w_in[20 + i]) for i in range(4)]
        U_g = [unit(w_in[12 + i]) for i in range(4)]
        U_wo = [unit(w_out[i]) for i in range(8)]
        U_gate, U_up, U_ada, U_dn = [], [], [], []
        for j in range(NF + 2):
            if j < NF:
                U_gate.append(unit(w_gu[j]))
                U_up.append(unit(w_gu[NF + j]))
            for _ in range(2):
                U_ada.append(unit(ada[len(U_ada)]))
            if j >= 2:
                U_dn.append(unit(w_down[j - 2]))
        U_rq = [unit(w_in2[i]) for i in range(4)]
        U_rk = [unit(w_in2[4 + i]) for i in range(4)]
        U_sq = [unit(w_in2[16 + i]) for i in range(4)]
        U_sk = [unit(w_in2[20 + i]) for i in range(4)]
        align()
        U_rv = [unit(w_in2[8 + i]) for i in range(4)]
        U_sv = [unit(w_in2[24 + i]) for i in range(4)]
        U_dec = [unit(decay[:, 0:1024]), unit(decay[:, 1024:2048])]
        U_rg = [unit(w_in2[12 + i]) for i in range(4)]
        U_wo2 = [unit(w_out2[i]) for i in range(8)]
        U_wq = [unit(w_q[i]) for i in range(16)]
        U_sub = [unit(subk[:, 0:1024]), unit(subk[:, 1024:2048])]

        hk = lambda k: hT[:, k * T:(k + 1) * T]
        xk = lambda k: xn[:, k * T:(k + 1) * T]

        def rms(src_t, scale_cols, dst, shift_cols=None, t_free=()):
            tq = [act(sq[:, i * 1024:(i + 1) * 1024], hT[:, i * 1024:(i + 1) * 1024], ACT.Square, *src_t)
                  for i in range(2)]
            b = bank(7)
            for k in range(KD):
                P.wait(tq[k // 4])
                tk = mm(pb[b][:, 0:T], c_("ones"), sq[:, k * T:(k + 1) * T], k == 0, k == KD - 1, sig=k == KD - 1)
            ta = act(stdt[:, 0:T], pb[b][:, 0:T], ACT.Sqrt, tk, scale=1.0 / D, bias=c_("eps"))
            readers[b] = [ta]
            tr = recip(rstd[:, 0:T], stdt[:, 0:T], ta)
            done = []
            for k in range(KD):
                t1 = stt(dst(k), hk(k), scale_cols(k), rstd[:, 0:T], MUL, MUL, tr, *src_t, *t_free)
                if shift_cols is not None:
                    t1 = ts(dst(k), dst(k), shift_cols(k), ADD, t1)
                done.append(t1)
            return done

        ang, kk_, rr_ = sq[:, 0:T], sq[:, T:2 * T], sq[:, 2 * T:3 * T]
        MAGIC = 12582912.0
        t = vcopy(ang, posi[:, :], L_pos)
        t = ts(ang, ang, c_("invf"), MUL, t)
        t = ts(kk_, ang, 1.0 / (2 * math.pi), MUL, t, s2=MAGIC, op1=ADD)
        t = ts(kk_, kk_, -MAGIC, ADD, t)
        c1 = 6.28125
        c2 = float(np.float32(round((2 * math.pi - c1) * 2 ** 21) / 2 ** 21))
        c3 = 2 * math.pi - c1 - c2
        for cc in (c1, c2, c3):
            t = stt(ang, kk_, -cc, ang, MUL, ADD, t)
        PI_ = 3.1415925
        t = ts(ang, ang, PI_, MIN, t, s2=-PI_, op1=MAX)
        t1 = act(sinT[:, :], ang, ACT.Sin, t)
        t2 = act(rr_, ang, ACT.Sin, t, scale=0.5)
        t = tt(rr_, rr_, rr_, MUL, t2)
        t_cos = ts(cosT[:, :], rr_, -2.0, MUL, t, s2=1.0, op1=ADD)
        t_rope = [t1, t_cos]

        lbm, e0, e1, lbd, oml = (small[:, 4 * i:4 * i + 4] for i in range(5))
        sp, su, sp_acc, nsp, cs8 = (small[:, 20 + 8 * i:20 + 8 * i + (8 if i == 4 else 4)] for i in range(5))
        t = tt(lbm, vc("lb0", 0, 4), vc("lb1", 0, 4), MAX)
        ta = tt(e0, vc("lb0", 0, 4), lbm, SUB, t)
        tb = tt(e1, vc("lb1", 0, 4), lbm, SUB, t)
        t_ = ts(sp, vc("la", 0, 4), -1.0, MUL)
        t_ = tt(su, vc("la", 0, 4), sp, MAX, t_)
        A.quiet(lambda e: e.preload_act_table_set("natural_log_exp_and_others"))
        ta = act(e0, e0, ACT.Exp, ta)
        tb = act(e1, e1, ACT.Exp, tb)
        te = act(su, su, ACT.Exp, t_, scale=-1.0)
        t = tt(e1, e0, e1, ADD, ta, tb)
        t = recip(e1, e1, t)
        t = tt(lbd, e0, e1, MUL, t)
        t_lb = ts(oml, lbd, -1.0, MUL, t, s2=1.0, op1=ADD)
        t = ts(sp_acc, su, 2.0, ADD, te)
        t = recip(sp_acc, sp_acc, t)
        t = tt(su, su, sp_acc, MUL, t)
        w2_ = small[:, 60:64]
        t = tt(w2_, su, su, MUL, t)
        t = ts(sp_acc, w2_, 1.0 / 17, MUL, t, s2=1.0 / 15, op1=ADD)
        for n in (13, 11, 9, 7, 5, 3, 1):
            t = tt(sp_acc, sp_acc, w2_, MUL, t)
            t = ts(sp_acc, sp_acc, 1.0 / n, ADD, t)
        t = tt(sp_acc, sp_acc, su, MUL, t)
        t = ts(sp, sp, 0.0, MAX, t)
        t = stt(sp, sp_acc, 2.0, sp, MUL, ADD, t)
        t_sp = ts(nsp, sp, -LRU_C, MUL, t)
        t = act(cs8, vc("c", 0, 8), ACT.Sigmoid)
        t_c = tt(cs8, cs8, vc("c", 0, 8), MUL, t)

        t_xn = rms([L_x, t_cos], lambda k: vc("mix", k), xk)
        xr = lambda k: xk(k)
        sf, ff, kk, lf, bb, eb, kdec, qs, qdec, vtok, kstT, scT = (blk(i) for i in range(12))
        Sst = arena[:, 12 * 1024:12 * 1024 + 3584]
        lx, xc, lg, gs = blk(16), blk(17), blk(18), blk(19)
        half = lambda ap, i: ap[:, i * 512:(i + 1) * 512]
        one_ = lambda ap, h: ap[:, h * T:(h + 1) * T]

        t_z = V.do(lambda e: e.memset(scT, 0.0))
        t_sf = []
        for i in range(2):
            b, tk = gemm(U_f[2 * i:2 * i + 2], xr, t_xn)
            t = act(half(sf, i), pb[b][:, :], ACT.Sigmoid, tk)
            readers[b] = [t]
            t_sf.append(t)
        t_qs = []
        for i in range(2):
            b, tk = gemm(U_qq[2 * i:2 * i + 2], xr)
            t = act(half(qs, i), pb[b][:, :], ACT.Sigmoid, tk)
            t = tt(half(qs, i), pb[b][:, :], half(qs, i), MUL, t)
            readers[b] = [t]
            t_qs.append(t)
        t_v = []
        for tile in range(2):
            b, tk = gemm_tok(U_i, xk, tile, last=tile == 1)
            t = act(half(vtok, tile), pb[b][:, :], ACT.Copy, tk)
            readers[b] = [t]
            t_v.append(t)
        t_f = [ts(one_(ff, h), one_(sf, h), oml[:, h:h + 1], MUL, t_sf[h // 2], t_lb, s2=lbd[:, h:h + 1], op1=ADD)
               for h in range(4)]
        t_k = ts(kk, ff, -1.0, MUL, *t_f, s2=1.0, op1=ADD)
        A.quiet(lambda e: e.preload_act_table_set("natural_log_exp_and_others"))
        t_lf = act(lf, ff, ACT.Ln, *t_f)
        t = V.do(lambda e: e.memset(sq[:, 0:1024], 1.0), *t_xn)
        t = V.do(lambda e: e.memset(sq[:, 0:1024:CH], 0.0), t)
        t_b = V.do(lambda e: e.tensor_tensor_scan(bb, sq[:, 0:1024], lf, 0.0, MUL, ADD), t, t_lf)
        bl = v3(bb, CH)[:, :, CH - 1:CH].broadcast_to([128, 32, CH])
        t_d = tt(v3(sf, CH), bl, v3(bb, CH), SUB, t_b, *t_f)
        t_eb = act(eb, bb, ACT.Exp, t_b)
        t = act(kdec, bb, ACT.Exp, t_b, scale=-1.0)
        t_ed = act(sf, sf, ACT.Exp, t_d)
        t_qd = tt(qdec, qs, eb, MUL, t_eb, *t_qs)
        t_kd = tt(kdec, kk, kdec, MUL, t, t_k)
        t_ks = tt(sf, kk, sf, MUL, t_ed, t_k)
        t_lx = []
        for i in range(2):
            b, tk = gemm(U_lx[2 * i:2 * i + 2], xr)
            t = act(half(lx, i), pb[b][:, :], ACT.Copy, tk)
            readers[b] = [t]
            t_lx.append(t)
        t_lg = []
        for i in range(2):
            b, tk = gemm(U_lg[2 * i:2 * i + 2], xr)
            t = act(half(lg, i), pb[b][:, :], ACT.Copy, tk)
            readers[b] = [t]
            t_lg.append(t)
        t_xc = []
        for j in range(4):
            t = ts(one_(xc, j), one_(lx, j), vc("conv", 12 + j), MUL, t_lx[j // 2], s2=vc("convb", j), op1=ADD)
            for tap in (2, 1, 0):
                s = 3 - tap
                t = stt(xc[:, j * T + s:(j + 1) * T], lx[:, j * T:(j + 1) * T - s], vc("conv", tap * 4 + j),
                        xc[:, j * T + s:(j + 1) * T], MUL, ADD, t)
            t_xc.append(t)
        t_kT = []
        for tile in range(2):
            b = bank(4 + tile)
            for h in range(4):
                fn = lambda e, o=pb[b][:, h * 128:(h + 1) * 128], i=sf[:, h * T + tile * 128:h * T + tile * 128 + 128]: \
                    e.transpose(o, i, c_("ident"))
                tk = P.do(fn, t_ks)
            t = act(half(kstT, tile), pb[b][:, :], ACT.Copy, tk)
            readers[b] = [t]
            t_kT.append(t)
        t_sc = []
        hgm = c_("hgm").bitcast(U32).unsqueeze(1).broadcast_to([128, 4, 128])
        for tile in range(2):
            b = bank(6 + tile)
            for h in range(4):
                s = slice(h * T + tile * 128, h * T + tile * 128 + 128)
                tk = mm(pb[b][:, h * 128:(h + 1) * 128], kdec[:, s], qdec[:, s], True, True, t_kd, t_qd, sig=True)
            t = V.do(lambda e, o=v3(half(scT, tile), 128), i=v3(pb[b][:, :], 128): e.copy_predicated(o, hgm, i), tk, t_z)
            readers[b] = [t]
            t_sc.append(t)
        t_gs = []
        for i in range(2):
            b, tk = gemm(U_g[2 * i:2 * i + 2], xr)
            t = act(half(gs, i), pb[b][:, :], ACT.Sigmoid, tk)
            t = tt(half(gs, i), pb[b][:, :], half(gs, i), MUL, t)
            readers[b] = [t]
            t_gs.append(t)
        t_win = tk
        rg_, ig_ = ff, lf
        t_r, t_ig = [], []
        for gi, (dst, bias, lst) in enumerate(((rg_, "ba", t_r), (ig_, "bx", t_ig))):
            for i in range(2):
                b = bank()
                for jj in range(2):
                    j = 2 * i + jj
                    tk = mm(pb[b][:, jj * T:(jj + 1) * T], slot(U_lw)[:, (gi * 4 + j) * 128:(gi * 4 + j + 1) * 128],
                            one_(xc, j), True, True, landed(U_lw), t_xc[j], sig=True)
                for jj in range(2):
                    j = 2 * i + jj
                    t = act(one_(dst, j), pb[b][:, jj * T:(jj + 1) * T], ACT.Sigmoid, tk, t_k, t_b, bias=vc(bias, j))
                    lst.append(t)
                readers[b] = [t]
        freed[U_lw] = tk
        gx = sq[:, 1024:2048]
        t = tt(gx, lg, lg, MUL, *t_lg, *t_xn)
        t = ts(gx, gx, 0.044715, MUL, t, s2=1.0, op1=ADD)
        t = tt(gx, gx, lg, MUL, t)
        t = act(gx, gx, ACT.Tanh, t, scale=math.sqrt(2.0 / math.pi))
        t = stt(gx, gx, 1.0, lg, ADD, MUL, t)
        t_gl = ts(gx, gx, 0.5, MUL, t)
        la_, th_, a_ = kk, lx, ff
        t_la = [ts(one_(la_, j), one_(rg_, j), nsp[:, j:j + 1], MUL, t_r[j], t_sp, t_kd, t_ks) for j in range(4)]
        t_th = act(th_, la_, ACT.Tanh, *t_la, *t_xc, scale=-1.0)
        t_a = act(a_, la_, ACT.Exp, *t_la)
        t_i = tt(ig_, ig_, xc, MUL, *t_ig)
        t = tt(la_, a_, a_, MUL, t_a, t_th)
        t = stt(la_, la_, 1.0, th_, ADD, MUL, t)
        t = act(la_, la_, ACT.Sqrt, t)
        t_bi = tt(la_, la_, ig_, MUL, t, t_i)
        t = V.do(lambda e: e.memset(a_[:, 0:1024:T], 0.0), t_bi)
        t_h = V.do(lambda e: e.tensor_tensor_scan(th_, a_, la_, 0.0, MUL, ADD), t)
        t_y = tt(xn[:, 1024:2048], th_, gx, MUL, t_h, t_gl, t_win)
        t_S = [None] * NCH
        for c in range(NCH - 1):
            b = bank(4 + c % 2)
            tile, r = c // 4, 32 * (c % 4)
            for h in range(4):
                tk = mm(pb[b][:, h * 128:(h + 1) * 128], kstT[r:r + 32, tile * 512 + h * 128:tile * 512 + h * 128 + 128],
                        vtok[r:r + 32, tile * 512 + h * 128:tile * 512 + h * 128 + 128], True, True,
                        t_kT[tile], t_v[tile], sig=h == 3)
            new = Sst[:, c * 512:(c + 1) * 512]
            if c == 0:
                t = vcopy(new, pb[b][:, :], tk)
            else:
                old = Sst[:, (c - 1) * 512:c * 512]
                for h in range(4):
                    hs = slice(h * 128, (h + 1) * 128)
                    t = stt(new[:, hs], old[:, hs], eb[:, h * T + c * CH + CH - 1:h * T + c * CH + CH],
                            pb[b][:, hs], MUL, ADD, tk, t_S[c], t_eb)
            readers[b] = [t]
            t_S[c + 1] = t
        t_o = []
        for hp in range(2):
            b = bank(6 + hp)
            for hh in range(2):
                h = 2 * hp + hh
                for tile in range(2):
                    mm(pb[b][:, hh * T + tile * 128:hh * T + tile * 128 + 128],
                       vtok[:, tile * 512 + h * 128:tile * 512 + h * 128 + 128],
                       scT[:, tile * 512 + h * 128:tile * 512 + h * 128 + 128], hh == 0 and tile == 0, False,
                       t_sc[tile], t_v[tile], skip=True)
        for c in range(1, NCH):
            for h in range(4):
                b = 6 + h // 2
                tk = mm(pb[b][:, (h % 2) * T + c * CH:(h % 2) * T + (c + 1) * CH],
                        Sst[:, (c - 1) * 512 + h * 128:(c - 1) * 512 + (h + 1) * 128],
                        qdec[:, h * T + c * CH:h * T + (c + 1) * CH], False, c == NCH - 1, t_S[c],
                        sig=c == NCH - 1, skip=True)
        for hp in range(2):
            b = 6 + hp
            t = act(half(sq, hp), pb[b][:, :], ACT.Square, tk, t_b)
            bs = bank()
            ts_ = mm(pb[bs][:, :], c_("ones"), half(sq, hp), True, True, t, sig=True)
            t = act(stdt[:, :], pb[bs][:, :], ACT.Sqrt, ts_, scale=1.0 / 128, bias=c_("eps"))
            readers[bs] = [t]
            tr = recip(rstd[:, :], stdt[:, :], t)
            t = stt(half(xn, hp), pb[b][:, :], vc("hgn"), rstd[:, :], MUL, MUL, tr, t_win)
            readers[b] = [t]
            t = tt(half(xn, hp), half(xn, hp), half(gs, hp), MUL, t, t_gs[hp])
            A.wait(t)
        t_mix = [t, t_y]

        def residual(us, rhs, t, gate=None):
            done = []
            for i in range(4):
                b, tk = gemm(us[2 * i:2 * i + 2], rhs, t)
                if gate is None:
                    tv = tt(hT[:, i * 512:(i + 1) * 512], hT[:, i * 512:(i + 1) * 512], pb[b][:, :], ADD, tk)
                else:
                    for j in range(2):
                        k = 2 * i + j
                        tv = stt(hk(k), pb[b][:, j * T:(j + 1) * T], gate(k), hk(k), MUL, ADD, tk)
                readers[b] = [tv]
                done.append(tv)
            return done, tk

        t_h1, tp = residual(U_wo, xk, t_mix)

        t_xn = rms(t_h1, lambda k: vc("ffn", k), xk, t_free=(tp,))
        acts = arena[:, 0:NF * T]
        sgm = [arena[:, 6 * 1024 + i * T:6 * 1024 + (i + 1) * T] for i in range(4)]
        ringset[0] = [0, 1, 2]
        b_ada = bank(3)
        for b in range(4, 8):
            bank(b)
        t_act = []

        def ada_cols(us):
            for u in us:
                n = U_ada.index(u)
                for k in range(KD):
                    tk = mm(pb[b_ada][:, n:n + 1], slot(u)[:, k * 128:(k + 1) * 128], cs8[:, k:k + 1],
                            k == 0, k == KD - 1, landed(u), t_c, sig=k == KD - 1)
                freed[u] = tk
            return tk

        for j in range(NF + 2):
            if j < NF:
                b, tk = gemm([U_gate[j], U_up[j]], xk, t_xn)
                s = sgm[j % 4]
                t = act(s, pb[b][:, 0:T], ACT.Sigmoid, tk, *(t_act[j - 4:j - 3] if j >= 4 else t_xn))
                t = tt(s, pb[b][:, 0:T], s, MUL, t)
                t = tt(acts[:, j * T:(j + 1) * T], s, pb[b][:, T:2 * T], MUL, t)
                readers[b] = [t]
                t_act.append(t)
            t_ada = ada_cols(U_ada[2 * j:2 * j + 2])
            if j >= 2:
                k = j - 2
                u = U_dn[k]
                P.wait(landed(u), t_act[k])
                for n in range(8):
                    tk = mm(pb[4 + n // 2][:, (n % 2) * T:(n % 2 + 1) * T], slot(u)[:, n * 128:(n + 1) * 128],
                            acts[:, k * T:(k + 1) * T], k == 0 and n % 2 == 0, k == NF - 1, sig=n == 7, skip=True)
                freed[u] = tk
        t_dn = tk
        mod = small[:, 64:112]
        t_mod = tt(mod, pb[b_ada][:, 0:48], vc("adab", 0, 48), ADD, t_ada)
        readers[b_ada] = [t_mod]
        g1s, g2s = small[:, 112:120], small[:, 120:128]
        t1 = stt(g1s, mod[:, 8:16], 1.0, vc("n1", 0, 8), ADD, MUL, t_mod)
        t2 = stt(g2s, mod[:, 32:40], 1.0, vc("n2", 0, 8), ADD, MUL, t_mod)
        t_mods = [t1, t2, t_mod]
        done = []
        for i in range(4):
            t = tt(hT[:, i * 512:(i + 1) * 512], hT[:, i * 512:(i + 1) * 512], pb[4 + i][:, :], ADD, t_dn, *t_xn)
            readers[4 + i] = [t]
            done.append(t)
        ringset[0] = [0, 1, 2, 3]
        t_x1 = rms(done, lambda k: vc("fin", k), hk)
        t_xn = rms(t_x1, lambda k: g1s[:, k:k + 1], xk, lambda k: mod[:, k:k + 1], t_free=(*t_mods, t_dn))
        rq, rk, rq2, rk2, sbq, sbk, rv, sv, rgs, tm1, tm2 = (blk(i) for i in range(11))
        scR = [arena[:, 11 * 1024 + i * 384:11 * 1024 + (i + 1) * 384] for i in range(4)]
        yr, ys = blk(13), blk(19)
        cb = cosT[:, :].unsqueeze(1).broadcast_to([128, 2, T])
        sb_ = sinT[:, :].unsqueeze(1).broadcast_to([128, 2, T])

        def rope(us, raw, dst):
            done = []
            for i in range(2):
                b, tk = gemm(us[2 * i:2 * i + 2], xr, t_xn)
                t = act(half(raw, i), pb[b][:, :], ACT.Copy, tk)
                readers[b] = [t]
                b2 = bank()
                tk = mm(pb[b2][:, :], c_("rot"), half(raw, i), True, True, t, sig=True)
                ta = tt(v3(half(dst, i), T), v3(half(raw, i), T), cb, MUL, t, *t_rope)
                t = tt(v3(half(raw, i), T), v3(pb[b2][:, :], T), sb_, MUL, tk, ta)
                readers[b2] = [t]
                done.append(tt(half(dst, i), half(dst, i), half(raw, i), ADD, t))
            return done

        def group_rms(src, tmp, gain, i, t):
            tq = act(half(tmp, i), half(src, i), ACT.Square, *t)
            b = bank()
            tk = mm(pb[b][:, :], c_("bd64"), half(tmp, i), True, True, tq, sig=True)
            ta = act(half(tmp, i), pb[b][:, :], ACT.Sqrt, tk, bias=c_("eps"))
            readers[b] = [ta]
            tr = recip(half(tmp, i), half(tmp, i), ta)
            return stt(half(src, i), half(src, i), gain, half(tmp, i), MUL, MUL, tr)

        t_rq = rope(U_rq, rq, rq2)
        t_rk = rope(U_rk, rk, rk2)
        raw = {}
        for name, us, dst in (("q", U_sq, sbq), ("k", U_sk, sbk)):
            raw[name] = []
            for i in range(2):
                b, tk = gemm(us[2 * i:2 * i + 2], xr)
                t = act(half(dst, i), pb[b][:, :], ACT.Copy, tk)
                readers[b] = [t]
                raw[name].append(t)
        t_sq = [group_rms(sbq, tm1, vc("sbq"), i, [raw["q"][i]]) for i in range(2)]
        t_sk = [group_rms(sbk, tm2, vc("sbk"), i, [raw["k"][i]]) for i in range(2)]
        t_tok = {}
        for name, us, dst in (("r", U_rv, rv), ("s", U_sv, sv)):
            t_tok[name] = []
            for tile in range(2):
                b, tk = gemm_tok(us, xk, tile, last=tile == 1)
                t = act(half(dst, tile), pb[b][:, :], ACT.Copy, tk)
                readers[b] = [t]
                t_tok[name].append(t)
        t_rg = []
        for i in range(2):
            b, tk = gemm(U_rg[2 * i:2 * i + 2], xr)
            t = act(half(rgs, i), pb[b][:, :], ACT.Sigmoid, tk)
            t = tt(half(rgs, i), pb[b][:, :], half(rgs, i), MUL, t)
            readers[b] = [t]
            t_rg.append(t)
        t_win2 = tk

        def head_scores(kT, qT, h, t):
            r, j = 64 * (h % 2), h // 2
            b = bank()
            mm(pb[b][:, 0:T], kT[r:r + 64, j * T:j * T + 128], qT[r:r + 64, j * T:(j + 1) * T], True, True, *t)
            tk = mm(pb[b][:, T:T + 128], kT[r:r + 64, j * T + 128:(j + 1) * T], qT[r:r + 64, j * T + 128:(j + 1) * T],
                    True, True, sig=True)
            return b, tk

        def head_out(w, v, h, b, t):
            r, o = 64 * (h % 2), (h // 2 % 2) * T
            mm(pb[b][r:r + 64, o:o + T], v[:, h * 64:(h + 1) * 64], w[:, 0:T], True, False, *t, skip=True)
            return mm(pb[b][r:r + 64, o + 128:o + T], v[:, 512 + h * 64:512 + (h + 1) * 64], w[:, T:T + 128],
                      False, True, sig=True, skip=True)

        t_scR, t_yr = [], []
        for i in range(8 + 1):
            if i < 8:
                h = i
                b, tk = head_scores(rk2, rq2, h, [*t_rq, *t_rk])
                dec = slot(U_dec[h // 4])[:, (h % 4) * T:(h % 4 + 1) * T]
                w = scR[h % 4]
                fr = t_yr[h - 4:h - 3] if h >= 4 else []
                tt(w[:, 0:T], pb[b][:, 0:T], dec, MUL, tk, landed(U_dec[h // 4]), *fr)
                t = tt(w[:, T:T + 128], pb[b][:, T:T + 128], dec[:, 0:128], MUL)
                readers[b] = [t]
                t_scR.append(t)
                freed[U_dec[h // 4]] = t
            if i >= 1:
                h = i - 1
                if h % 4 == 0:
                    bank(4 + h // 4)
                t_yr.append(head_out(scR[h % 4], rv, h, 4 + h // 4, [t_scR[h], *t_tok["r"]]))
        t_ret = []
        for i in range(2):
            t = act(half(yr, i), pb[4 + i][:, :], ACT.Copy, t_yr[4 * i + 3])
            readers[4 + i] = [t]
            b = bank()
            tk = mm(pb[b][:, :], c_("bd64"), half(yr, i), True, True, t, sig=True)
            t = tt(half(yr, i), half(yr, i), pb[b][:, :], SUB, tk)
            readers[b] = [t]
            tq = act(half(tm1, i), half(yr, i), ACT.Square, t, t_sq[i])
            b = bank()
            tk = mm(pb[b][:, :], c_("bd64"), half(tm1, i), True, True, tq, sig=True)
            ta = act(half(tm1, i), pb[b][:, :], ACT.Sqrt, tk, bias=c_("eps"))
            readers[b] = [ta]
            tr = recip(half(tm1, i), half(tm1, i), ta)
            for j in range(2):
                k = 2 * i + j
                t = stt(one_(yr, k), one_(yr, k), vc("retg", k), one_(tm1, k), MUL, MUL, tr)
                t = tt(xk(k), one_(yr, k), one_(rgs, k), MUL, t, t_rg[i], t_win2)
                t_ret.append(t)
        az = [arena[:, 14 * 1024 + i * 384:14 * 1024 + (i + 1) * 384] for i in range(3)]
        be = [arena[:, 14 * 1024 + (3 + i) * 384:14 * 1024 + (4 + i) * 384] for i in range(3)]
        st = [arena[:, 14 * 1024 + (6 + i) * 384:14 * 1024 + (7 + i) * 384] for i in range(3)]
        sbm = c_("sbm").unsqueeze(1).broadcast_to([128, 2, 128])

        def diag(ap):
            return bass.AP(ap.tensor, ap.offset, [ap.ap[0], [256, 2], [1, 128]])

        t_be, t_st, t_w, t_ys, cumtk = {}, {}, {}, {}, {}
        A.quiet(lambda e: e.preload_act_table_set("natural_log_exp_and_others"))
        for i in range(8 + 2):
            if i < 8:
                h, n = i, i % 3
                b, tk = head_scores(sbk, sbq, h, [*t_sq, *t_sk])
                fr = [t_ys[h - 3]] if h >= 3 else []
                t_abs = act(az[n], pb[b][:, 0:384], ACT.Abs, tk, *fr, scale=0.125)
                t = act(az[n], az[n], ACT.Exp, t_abs, scale=-1.0)
                t = act(az[n], az[n], ACT.Ln, t, bias=c_("one"))
                tb = ts(be[n], pb[b][:, 0:384], 0.125, MUL, t_abs, *([t_w[h - 3]] if h >= 3 else []), s2=0.0, op1=MIN)
                tb = tt(be[n], be[n], az[n], SUB, tb, t)
                t = stt(st[n], pb[b][:, 0:384], -0.125, be[n], MUL, ADD, tb, *([cumtk[h - 3]] if h >= 3 else []))
                readers[b] = [t]
                t_be[h] = tb
                t_st[h] = tt(diag(st[n]), diag(st[n]), sbm, MUL, t)
            if 1 <= i <= 8:
                h, n = i - 1, (i - 1) % 3
                b = bank()
                mm(pb[b][:, 0:384], c_("tri"), st[n], True, False, t_st[h], skip=True)
                tk = mm(pb[b][:, 128:256], c_("ones"), st[n][:, 256:384], False, True, sig=True, skip=True)
                cumtk[h] = tk
                t = tt(be[n], be[n], pb[b][:, 0:384], ADD, tk, t_be[h])
                readers[b] = [t]
                t = act(az[n], be[n], ACT.Exp, t)
                t_w[h] = tt(diag(az[n]), diag(az[n]), sbm, MUL, t)
            if i >= 2:
                h, n = i - 2, (i - 2) % 3
                if h % 4 == 0:
                    bank(6 + h // 4)
                t_ys[h] = head_out(az[n], sv, h, 6 + h // 4, [t_w[h], *t_tok["s"]])
        t_sb = []
        for i in range(2):
            t = act(half(ys, i), pb[6 + i][:, :], ACT.Copy, t_ys[4 * i + 3])
            readers[6 + i] = [t]
            t = group_rms(ys, tm2, vc("sbo"), i, [t, t_sk[i]])
            t_sb.append(vcopy(xn[:, 1024 + i * 512:1024 + (i + 1) * 512], half(ys, i), t, t_win2))

        t_x2, tp = residual(U_wo2, xk, [*t_ret, *t_sb], gate=lambda k: mod[:, 16 + k:17 + k])

        t_xn = rms(t_x2, lambda k: g2s[:, k:k + 1], xk, lambda k: mod[:, 24 + k:25 + k], t_free=(tp,))
        qry = arena[:, 0:4096]
        h2t = [blk(4), blk(5)]
        x2t = [blk(6), blk(7)]
        g2b = blk(8)
        SC = [arena[:, (9 + 2 * i) * 1024:(11 + 2 * i) * 1024] for i in range(2)]
        pk = arena[:, 13 * 1024:16 * 1024]
        dgr = [arena[:, 16 * 1024 + i * 128:16 * 1024 + (i + 1) * 128] for i in range(16)]
        fo = blk(18)
        idsb = sb("idsb", 256, U32)
        tiu = sb("tiu", 32, U32)
        bcu = sb("bcu", 16, U32)
        abu = sb("abu", 32, U32)
        t_qry = []
        for i in range(8):
            b, tk = gemm(U_wq[2 * i:2 * i + 2], xk, t_xn)
            t = act(qry[:, i * 512:(i + 1) * 512], pb[b][:, :], ACT.Copy, tk, *t_ret, *t_sb)
            readers[b] = [t]
            t_qry.append(t)
        t_SC = [[], []]
        for tile in range(2):
            for g in range(4):
                b = bank()
                for n in range(4):
                    hp = 4 * g + n
                    tk = mm(pb[b][:, n * 128:(n + 1) * 128], qry[:, hp * T + tile * 128:hp * T + tile * 128 + 128],
                            slot(U_sub[hp // 8])[:, (hp % 8) * 128:(hp % 8 + 1) * 128], True, True,
                            t_qry[hp // 2], landed(U_sub[hp // 8]), sig=n == 3)
                    freed[U_sub[hp // 8]] = tk
                t = act(SC[tile][:, g * 512:(g + 1) * 512], pb[b][:, :], ACT.Copy, tk)
                readers[b] = [t]
                t_SC[tile].append(t)
        freed[U_sub[0]] = freed[U_sub[1]] = tk
        t_h2t, t_x2t = [[], []], [[], []]
        for src, dst, lst, t0 in ((xk, h2t, t_h2t, t_xn), (hk, x2t, t_x2t, t_x2)):
            for tile in range(2):
                for g in range(2):
                    b = bank()
                    for n in range(4):
                        fn = lambda e, o=pb[b][:, n * 128:(n + 1) * 128], \
                            i=src(4 * g + n)[:, tile * 128:(tile + 1) * 128]: e.transpose(o, i, c_("ident"))
                        tk = P.do(fn, *t0)
                    t = act(dst[tile][:, g * 512:(g + 1) * 512], pb[b][:, :], ACT.Copy, tk)
                    readers[b] = [t]
                    lst[tile].append(t)
        t_g2 = []
        dg = sq[:, 0:1024]
        for g in range(2):
            b = bank()
            for n in range(4):
                k = 4 * g + n
                t = ts(dg[:, k * 128:(k + 1) * 128], c_("ident"), mod[:, 40 + k:41 + k], MUL, *t_xn)
                tk = mm(pb[b][:, n * 128:(n + 1) * 128], c_("ones"), dg[:, k * 128:(k + 1) * 128], True, True, t, sig=True)
            t = act(g2b[:, g * 512:(g + 1) * 512], pb[b][:, :], ACT.Copy, tk)
            readers[b] = [t]
            t_g2.append(t)

        f32c = lambda o, n: pk[:, o:o + n]
        tsv, tif, abf, iab = f32c(0, 32), f32c(32, 32), f32c(64, 32), f32c(96, 32)
        bsv, nb, ssum = f32c(128, 16), f32c(144, 1), f32c(145, 1)
        sc2 = f32c(160, 256)
        cand, cand2 = f32c(416, 256), f32c(672, 256)
        eq = f32c(928, 512)
        gts, aa, ae, ex = f32c(1440, 256), f32c(1696, 256), f32c(1952, 256), f32c(2208, 256)

        def top16(src, tmp, vals, idx, *t):
            t1 = V.do(lambda e: e.max(vals[:, 0:8], src), *t)
            V.do(lambda e: e.max_index(idx[:, 0:8], vals[:, 0:8], src), t1)
            t1 = V.do(lambda e: e.match_replace(tmp, vals[:, 0:8], src, NEG), t1)
            t1 = V.do(lambda e: e.max(vals[:, 8:16], tmp), t1)
            return V.do(lambda e: e.max_index(idx[:, 8:16], vals[:, 8:16], tmp), t1)

        t_ids, t_gt = {}, {}

        def choose(n):
            tile, h = n // 8, n % 8
            for p in range(2):
                s = SC[tile][:, (2 * h + p) * 128:(2 * h + p + 1) * 128]
                t = top16(s, sc2[:, 0:128], tsv[:, p * 16:p * 16 + 16], tiu[:, p * 16:p * 16 + 16],
                          t_SC[tile][h // 2], (V.sem, V.n))
            tf = vcopy(tif, tiu[:, :], t)
            t = tt(v3(cand, 16), tsv[:, 0:16].unsqueeze(2).broadcast_to([128, 16, 16]),
                   tsv[:, 16:32].unsqueeze(1).broadcast_to([128, 16, 16]), ADD, t)
            exn = ex[:, n * 16:(n + 1) * 16]
            t = top16(cand, cand2, bsv, bcu[:, :], t, *([t_gt[n - 1][0]] if n else []))
            tn = ts(nb, bsv[:, 0:1], -1.0, MUL, t)
            te = act(exn, bsv, ACT.Exp, tn, bias=nb, accum_out=ssum)
            ta = V.do(lambda e: e.tensor_scalar(abu[:, 0:16], bcu[:, :], 4, None, ALU.logical_shift_right), t)
            tb = V.do(lambda e: e.tensor_scalar(abu[:, 16:32], bcu[:, :], 15, None, ALU.bitwise_and), t)
            t = vcopy(abf, abu[:, :], ta, tb)
            t = tt(v3(eq, 16), c_("iota").unsqueeze(1).broadcast_to([128, 32, 16]),
                   abf.unsqueeze(2).broadcast_to([128, 32, 16]), ALU.is_equal, t)
            e4 = eq.rearrange("p (a s m) -> p a s m", a=2, m=16)
            t = tt(e4, e4, tif.rearrange("p (a m) -> p a m", a=2).unsqueeze(2).broadcast_to([128, 2, 16, 16]), MUL, t, tf)
            t = V.do(lambda e: e.tensor_reduce(iab, v3(eq, 16), AX_X, ADD), t)
            t_ids[n] = stt(idsb[:, n * 16:(n + 1) * 16], iab[:, 0:16], 128.0, iab[:, 16:32], MUL, ADD, t)
            tr = recip(ssum, ssum, te)
            t = ts(gts[:, n * 16:(n + 1) * 16], exn, ssum, MUL, tr)
            t_gt[n] = (te, t)

        slot_free, slot_uses = {}, {}
        for s in range(SLOTS):
            us = [u for u in range(len(units)) if u % SLOTS == s and units[u] is not None]
            slot_free[s] = [freed[us[-1]]]
            slot_uses[s] = 0
        nxt = [0]

        def gather(table, col, tk_ids):
            s = nxt[0] % SLOTS
            nxt[0] += 1
            o = ring_sb[:, s * 1024:(s + 1) * 1024]
            slot_uses[s] += 1
            G.quiet(lambda e: e.indirect_dma_start(
                o, None, table, bass.IndirectOffsetOnAxis(ap=idsb[:, col:col + 1], axis=0)).then_inc(s_row[s], 16),
                tk_ids, *slot_free[s])
            slot_free[s] = None
            return s, o, (s_row[s], 16 * slot_uses[s])

        NB = 32
        choose(0)
        choose(1)
        downs, ups = {}, {}
        for b in range(4, 8):
            bank(b)
        t_dg = [None] * 256
        t_mmu = [None] * 256
        t_fo = None
        for i in range(NB + 1):
            if i < NB:
                downs[i] = [gather(peer_down, i * 8 + j, t_ids[i // 2]) for j in range(8)]
                tile = i // 16
                for j in range(8):
                    s, o, tl = downs[i][j]
                    col = i * 8 + j
                    t = V.do(lambda e, o=o, col=col, tile=tile: e.tensor_tensor_reduce(
                        o, o, h2t[tile], 1.0, 0.0, MUL, ADD, aa[:, col:col + 1]), tl, *t_h2t[tile])
                    slot_free[s] = [t]
                cols = slice(i * 8, i * 8 + 8)
                te = act(ae[:, cols], aa[:, cols], ACT.Gelu, t)
                if i % 2 == 0 and i // 2 + 2 < 16:
                    choose(i // 2 + 2)
                t = tt(ae[:, cols], ae[:, cols], gts[:, cols], MUL, te, t_gt[i // 2][1])
                for j in range(8):
                    col = i * 8 + j
                    fr = [t_mmu[col - 16]] if col >= 16 else []
                    t_dg[col] = act(dgr[col % 16], c_("ident"), ACT.Copy, t, *fr, scale=ae[:, col:col + 1])
                ups[i] = None
            if i >= 0 and i < NB:
                ups[i] = [gather(peer_up, i * 8 + j, t_ids[i // 2]) for j in range(8)]
                for j in range(8):
                    s, o, tl = ups[i][j]
                    col = i * 8 + j
                    first, last = col % 128 == 0, col % 128 == 127
                    mm(pb[4 + 2 * tile][:, :], dgr[col % 16], o[:, 0:512], first, last, tl, t_dg[col])
                    tk = mm(pb[5 + 2 * tile][:, :], dgr[col % 16], o[:, 512:1024], first, last, sig=True)
                    t_mmu[col] = tk
                    slot_free[s] = [tk]
                if i % 16 == 15:
                    for g in range(2):
                        gsl = slice(g * 512, (g + 1) * 512)
                        t = tt(fo[:, gsl], pb[4 + 2 * tile + g][:, :], g2b[:, gsl], MUL, tk, *t_g2,
                               *([t_fo] if t_fo else []))
                        t = tt(fo[:, gsl], fo[:, gsl], x2t[tile][:, gsl], ADD, t, *t_x2t[tile])
                    A.quiet(lambda e, tile=tile: e.dma_start(out[tile * 128:(tile + 1) * 128, :], fo).then_inc(s_out, 16), t)
                    t_fo = (s_out, 16 * (tile + 1))

        for u, src in enumerate(units):
            if src is None:
                continue
            prev = [x for x in range(u % SLOTS, u, SLOTS) if units[x] is not None]
            SY.quiet(lambda e, u=u, src=src: e.dma_start(slot(u), src).then_inc(s_slot[u % SLOTS], 16),
                     *([freed[prev[-1]]] if prev else []))
        SY.wait((s_out, 32))

        block = ctx.enter_context(nc.Block())

        @block.sync
        def _(e):
            SY.run(e)

        @block.gpsimd
        def _(e):
            G.run(e)

        @block.scalar
        def _(e):
            A.run(e)

        @block.vector
        def _(e):
            V.run(e)

        @block.tensor
        def _(e):
            P.run(e)


def kernel(**inputs):
    import numpy as _np
    import concourse.bacc as _bacc
    from concourse import mybir as _mybir
    from concourse.bass_utils import run_bass_kernel_spmd as _run

    a = {k: _np.asarray(v) for k, v in inputs.items()}

    def fm(v):
        return v.reshape(-1, 128).T

    def units(w):
        n = w.shape[1] // 128
        return _np.ascontiguousarray(w.reshape(8, 128, n, 128).transpose(2, 1, 0, 3)).reshape(n, 128, 1024)

    def twice(v):
        return _np.concatenate([v.reshape(-1), v.reshape(-1)]).reshape(128, 1)

    vecs = _np.concatenate([
        fm(a["mix_norm_w"]), fm(a["ffn_norm_w"]), fm(a["final_norm_w"]), fm(a["norm1_gain_2"]), fm(a["norm2_gain_2"]),
        fm(a["conv_w"][0]), fm(a["conv_b"]), fm(a["lru_ba"]), fm(a["lru_bx"]), fm(a["lru_a"]),
        fm(a["hg_lb"][0]), fm(a["hg_lb"][1]), fm(a["hg_norm_w"]), fm(a["ret_norm_gain_2"]),
        twice(a["sb_q_gain_2"]), twice(a["sb_k_gain_2"]), twice(a["sb_out_gain_2"]), fm(a["ada_b_2"]), fm(a["c_2"]),
    ], axis=1)
    lw = _np.zeros((128, 8, 128), _np.float32)
    for g, w in enumerate((a["lru_wa"][0], a["lru_wx"][0])):
        for j in range(4):
            lw[0:64, g * 4 + j, 0:64] = w[2 * j]
            lw[64:128, g * 4 + j, 64:128] = w[2 * j + 1]
    cst, dec = shape_constants()
    arrays = {
        "xT": a["x"][0].T.reshape(8, 128, 256).transpose(1, 0, 2).reshape(128, 2048),
        "vecs": vecs, "cst": cst, "decay": dec, "pos": a["positions_2"],
        "w_in": units(a["w_in"][0]), "w_out": units(a["w_out"][0]), "w_gu": units(a["w_gate_up"][0]),
        "w_down": a["w_down"][0].reshape(22, 128, 1024), "ada": units(a["ada_w_2"][0]),
        "w_in2": units(a["w_in_2"][0]), "w_out2": units(a["w_out_2"][0]), "w_q": units(a["peer_w_query_2"][0]),
        "subk": a["peer_sub_keys_2"][0].reshape(16, 128, 128).transpose(2, 0, 1).reshape(128, 2048),
        "lru_w": lw.reshape(128, 1024),
        "peer_down": a["peer_down_2"][0], "peer_up": a["peer_up_2"][0],
    }
    nc = _bacc.Bacc("TRN2", target_bir_lowering=False, num_devices=1)
    feed, args = {}, []
    for name, v in arrays.items():
        v = _np.ascontiguousarray(v)
        feed[f"in_{name}"] = v
        args.append(nc.dram_tensor(f"in_{name}", v.shape, _mybir.dt.from_np(v.dtype), kind="ExternalInput").ap())
    o = nc.dram_tensor("out_0", (256, 1024), _mybir.dt.float32, kind="ExternalOutput").ap()
    build(nc, *args, o)
    r = _run(nc, [feed], core_ids=[0])
    return r.results[0]["out_0"].reshape(1, 256, 1024)
```

```python
import math
from contextlib import ExitStack

import numpy as np

import concourse.bass as bass
from concourse import mybir

ALU = mybir.AluOpType
ACT = mybir.ActivationFunctionType
F32 = mybir.dt.float32
F32R = mybir.dt.float32r
U32 = mybir.dt.uint32
I32 = mybir.dt.int32
AX_X = mybir.AxisListType.X

T = 256
D = 1024
KD = D // 128
FF = 2816
NF = FF // 128
CH = 32
NCH = T // CH
LRU_C = 8.0
EPS = 1e-6
SLOTS = 16
WS = 6
NEXP = 16384
NEG = -3.0e38

VEC = {}
_at = 0
for _name, _n in (("mix", 8), ("ffn", 8), ("fin", 8), ("n1", 8), ("n2", 8), ("conv", 16), ("convb", 4), ("ba", 4),
                  ("bx", 4), ("la", 4), ("lb0", 4), ("lb1", 4), ("hgn", 1), ("retg", 4), ("sbq", 1), ("sbk", 1),
                  ("sbo", 1), ("adab", 48), ("c", 8)):
    VEC[_name] = (_at, _n)
    _at += _n
NVEC = _at

CST = {}
_at = 0
for _name, _n in (("ident", 128), ("rot", 128), ("ones", 128), ("bd64", 128), ("tri", 128), ("sbm", 128),
                  ("hgm", 128), ("iota", 16), ("invf", 1), ("eps", 1), ("one", 1), ("zero", 1)):
    CST[_name] = (_at, _n)
    _at += _n
NCST = _at


def shape_constants():
    c = np.zeros((128, NCST), np.float32)

    def put(name, a):
        s, n = CST[name]
        c[:, s:s + n] = np.asarray(a, np.float32).reshape(128, n)

    p = np.arange(128)
    put("ident", np.eye(128))
    rot = np.zeros((128, 128))
    for m in range(128):
        if m % 64 < 32:
            rot[m + 32, m] = -1.0
        else:
            rot[m - 32, m] = 1.0
    put("rot", rot)
    put("ones", np.ones((128, 128)))
    put("bd64", (p[:, None] // 64 == p[None, :] // 64) / 64.0)
    put("tri", p[:, None] > p[None, :])
    put("sbm", p[:, None] < p[None, :])
    put("hgm", (p[:, None] // CH == p[None, :] // CH) & (p[:, None] <= p[None, :]))
    put("iota", np.tile(np.arange(16), (128, 1)))
    put("invf", np.float32(10000.0) ** (-(p % 32).astype(np.float32) / np.float32(32)))
    put("eps", np.full(128, EPS))
    put("one", np.ones(128))
    dec = np.zeros((128, 8, T), np.float32)
    rel = np.arange(T)[None, :] - p[:, None]
    for h in range(8):
        lg = np.float32(np.log1p(-(2.0 ** (-5.0 - h))))
        dec[:, h] = np.where(rel >= 0, np.exp(np.float64(lg) * np.maximum(rel, 0)) * 0.125, 0.0)
    return c, dec.reshape(128, 8 * T)


class Queue:

    def __init__(self, sem):
        self.sem, self.n, self.items, self.past = sem, 0, [], {}

    def wait(self, *tickets):
        for sem, v in tickets:
            if self.past.get(sem.num, 0) < v:
                self.past[sem.num] = v
                self.items.append(lambda e, sem=sem, v=v: e.wait_ge(sem, v))

    def quiet(self, fn, *tickets):
        self.wait(*tickets)
        self.items.append(fn)

    def do(self, fn, *tickets):
        self.wait(*tickets)
        self.n += 1
        self.items.append(lambda e: fn(e).then_inc(self.sem, 1))
        return self.sem, self.n

    def run(self, eng):
        for f in self.items:
            f(eng)


def build(nc, xT, vecs, cst, decay, pos, w_in, w_out, w_gu, w_down, ada, w_in2, w_out2, w_q, subk, lru_w,
          peer_down, peer_up, out):
    ctx = ExitStack()
    with ctx:
        def sb(name, n, dt=F32):
            return ctx.enter_context(nc.sbuf_tensor(name, [128, n], dt))

        def sem(name):
            return ctx.enter_context(nc.semaphore(name))

        with nc.sbuf_tensor("ring_lo", [128, SLOTS * 1024], F32R) as ring_lo, \
                nc.sbuf_tensor("ahi", [128, 4 * T], F32R) as ahi, nc.sbuf_tensor("alo", [128, 4 * T], F32R) as alo:
            pass
        ring_sb = sb("ring_sb", SLOTS * 1024)
        subk_sb = sb("subk_sb", 2048)
        whi = sb("whi", WS * 1024, F32R)
        xhi = sb("xhi", 2048, F32R)
        xlo = sb("xlo", 2048, F32R)
        hT = sb("hT", 2048)
        xn = sb("xn", 2048)
        sq = sb("sq", 2048)
        cs = sb("cs", NCST)
        vv = sb("vv", NVEC)
        cosT = sb("cosT", T)
        sinT = sb("sinT", T)
        rstd = sb("rstd", 512)
        stdt = sb("stdt", 512)
        small = sb("small", 256)
        idsb = sb("idsb", 256, U32)
        tiu = sb("tiu", 32, U32)
        bcu = sb("bcu", 16, U32)
        abu = sb("abu", 32, U32)
        NBLK = 14
        arena = sb("arena", NBLK * 1024)
        pb = [ctx.enter_context(nc.psum_tensor(f"pb{i}", [128, 512], F32)) for i in range(8)]

        def blk(i, n=1024):
            return arena[:, i * 1024:i * 1024 + n]

        def v3(ap, m):
            return ap.rearrange("p (n m) -> p n m", m=m)

        def half(ap, i):
            return ap[:, i * 512:(i + 1) * 512]

        def one_(ap, h):
            return ap[:, h * T:(h + 1) * T]

        def c_(name):
            s, n = CST[name]
            return cs[:, s:s + n]

        def vc(name, j=0, n=1):
            s = VEC[name][0] + j
            return vv[:, s:s + n]

        P = Queue(sem("s_pe"))
        V = Queue(sem("s_dve"))
        A = Queue(sem("s_act"))
        G = Queue(sem("s_pool"))
        SY = Queue(sem("s_sp"))
        s_ld = [sem(f"s_ld{i}") for i in range(5)]
        s_slot = [sem(f"s_slot{i}") for i in range(SLOTS)]
        s_row = [sem(f"s_row{i}") for i in range(SLOTS)]
        s_out = sem("s_out")

        def act(o, i, f, *t, **kw):
            return A.do(lambda e: e.activation(o, i, f, **kw), *t)

        def tt(o, a, b, op, *t):
            return V.do(lambda e: e.tensor_tensor(o, a, b, op), *t)

        def ts(o, a, s1, op0, *t, s2=None, op1=None):
            if op1 is None:
                return V.do(lambda e: e.tensor_scalar(o, a, s1, None, op0), *t)
            return V.do(lambda e: e.tensor_scalar(o, a, s1, s2, op0, op1), *t)

        def stt(o, a, s, b, op0, op1, *t):
            return V.do(lambda e: e.scalar_tensor_tensor(out=o, in0=a, scalar=s, in1=b, op0=op0, op1=op1), *t)

        def vcopy(o, i, *t):
            return V.do(lambda e: e.tensor_copy(o, i), *t)

        def recip(o, i, *t):
            return V.do(lambda e: e.reciprocal(o, i), *t)

        def mm(o, l, r, start, stop, *t, sig=False, skip=False):
            fn = lambda e: e.matmul(o, l, r, start=start, stop=stop, skip_group_check=skip)
            return P.do(fn, *t) if sig else P.quiet(fn, *t)

        def table(name):
            A.quiet(lambda e: e.preload_act_table_set(name))

        MUL, ADD, SUB, MAX, MIN = ALU.mult, ALU.add, ALU.subtract, ALU.max, ALU.min
        LNEXP, SIGM = "natural_log_exp_and_others", "sigmoid_and_others"

        readers = [[] for _ in range(8)]
        turn = [0]
        ringset = [[0, 1, 2, 3]]

        def bank(i=None):
            if i is None:
                i = ringset[0][turn[0] % len(ringset[0])]
                turn[0] += 1
            P.wait(*readers[i])
            readers[i] = []
            return i

        units, freed = [], {}

        def unit(src):
            units.append(src)
            return len(units) - 1

        def slot(u):
            return ring_sb[:, (u % SLOTS) * 1024:(u % SLOTS + 1) * 1024]

        def landed(u):
            return s_slot[u % SLOTS], 16 * (u // SLOTS + 1)

        groups, ngroup, nsplit = [], [0], [0]
        wsp, wfree = {}, [[] for _ in range(WS)]

        def split_unit(u):
            s = nsplit[0] % WS
            hi, lo = whi[:, s * 1024:(s + 1) * 1024], ring_lo[:, (u % SLOTS) * 1024:(u % SLOTS + 1) * 1024]
            th = act(hi, slot(u), ACT.Copy, landed(u), *wfree[s])
            q = V if nsplit[0] % 4 == 3 or u in U_wq[4:] else G
            tl = q.do(lambda e: e.tensor_tensor(lo, slot(u), hi.bitcast(F32), SUB), landed(u), th)
            wsp[u] = (s, hi, lo, th, tl)
            nsplit[0] += 1

        def used(u, tk):
            wfree[wsp[u][0]] = [tk]
            freed[u] = [tk]
            held[0] -= 1

        held = [0]

        def take(us):
            assert groups[ngroup[0]] == us
            ngroup[0] += 1
            for g in range(ngroup[0] - 1, len(groups)):
                new = [u for u in groups[g] if u not in wsp]
                if held[0] + len(new) > WS:
                    break
                for u in new:
                    split_unit(u)
                held[0] += len(new)

        class Halves:

            def __init__(self, hi, lo):
                self.hi, self.lo, self.th, self.tl = hi, lo, {}, {}

        X = Halves(lambda k: one_(xhi, k), lambda k: one_(xlo, k))

        def split_x(k, src, t, h=X, slot_k=None, free=()):
            j = k if slot_k is None else slot_k
            h.th[k] = act(h.hi(j), src, ACT.Copy, t, *free)
            h.tl[k] = V.do(lambda e: e.tensor_tensor(h.lo(j), src, h.hi(j).bitcast(F32), SUB), h.th[k], t, *free)

        def products(o, u, c, ks, h, hk, start, stop, sig, skip=False):
            s, hi, lo, th, tl = wsp[u]
            P.wait(th)
            for i, k in enumerate(ks):
                mm(o, hi[:, c(k)], h.hi(hk(k)), start and i == 0, False, h.th[k], skip=skip)
                mm(o, hi[:, c(k)], h.lo(hk(k)), False, False, h.tl[k], skip=skip)
            for i, k in enumerate(ks):
                last = i == len(ks) - 1
                tk = mm(o, lo[:, c(k)], h.hi(hk(k)), False, stop and last, tl, sig=sig and last, skip=skip)
            return tk

        kc = lambda k: slice(k * 128, (k + 1) * 128)
        same = lambda k: k

        def gemm(us, b=None):
            take(us)
            b = bank(b)
            for i, u in enumerate(us):
                tk = products(one_(pb[b], i), u, kc, range(KD), X, same, True, True, True)
                used(u, tk)
            return b, tk

        def gemm_tok(us4):
            bs = [bank(), bank()]
            for p in range(2):
                us = us4[2 * p:2 * p + 2]
                take(us)
                for i, u in enumerate(us):
                    s, hi, lo, th, tl = wsp[u]
                    P.wait(th, tl)
                    for tile in range(2):
                        o = pb[bs[tile]][:, (2 * p + i) * 128:(2 * p + i + 1) * 128]
                        tok = slice(tile * 128, (tile + 1) * 128)
                        for k in range(KD):
                            mm(o, X.hi(k)[:, tok], hi[:, kc(k)], k == 0, False, X.th[k])
                            mm(o, X.hi(k)[:, tok], lo[:, kc(k)], False, False)
                            tk = mm(o, X.lo(k)[:, tok], hi[:, kc(k)], False, k == KD - 1, X.tl[k], sig=k == KD - 1)
                    used(u, tk)
            return bs, tk

        SY.quiet(lambda e: e.dma_start(hT[:, :], xT).then_inc(s_ld[1], 16))
        A.quiet(lambda e: e.dma_start(cs[:, :], cst).then_inc(s_ld[0], 16))
        A.quiet(lambda e: e.dma_start(vv[:, :], vecs).then_inc(s_ld[3], 16))
        posi = xn[:, 1024:1024 + T].bitcast(I32)
        A.quiet(lambda e: e.dma_start(posi, pos.to_broadcast([128, T])).then_inc(s_ld[2], 16))
        L_cst, L_x, L_pos, L_vec = (s_ld[0], 16), (s_ld[1], 16), (s_ld[2], 16), (s_ld[3], 16)

        def pairs(us):
            for i in range(0, len(us), 2):
                groups.append(us[i:i + 2])
            return us

        U_f = pairs([unit(w_in[4 + i]) for i in range(4)])
        U_qq = pairs([unit(w_in[i]) for i in range(4)])
        U_lx = pairs([unit(w_in[16 + i]) for i in range(4)])
        U_lw = unit(lru_w)
        U_i = pairs([unit(w_in[8 + i]) for i in range(4)])
        U_lg = pairs([unit(w_in[20 + i]) for i in range(4)])
        U_g = pairs([unit(w_in[12 + i]) for i in range(4)])
        U_wo = pairs([unit(w_out[i]) for i in range(8)])
        U_gate, U_up, U_ada, U_dn, ada_at = [], [], [], [], []
        for j in range(NF + 2):
            if j < NF:
                U_gate.append(unit(w_gu[j]))
                U_up.append(unit(w_gu[NF + j]))
                groups.append([U_gate[j], U_up[j]])
            n = len(U_ada)
            for _ in range(min(48 - n, 3)):
                k, c = len(U_ada) // 6, len(U_ada) % 6
                U_ada.append(unit(ada[k * 128:(k + 1) * 128, c * 1024:(c + 1) * 1024]))
            ada_at.append(range(n, len(U_ada)))
            if j >= 2:
                U_dn.append(unit(w_down[j - 2]))
                if j < NF:
                    groups.append([U_dn[j - 2]])
        groups.append(U_dn[NF - 2:])
        U_sq = pairs([unit(w_in2[16 + i]) for i in range(4)])
        U_sk = pairs([unit(w_in2[20 + i]) for i in range(4)])
        U_sv = pairs([unit(w_in2[24 + i]) for i in range(4)])
        U_rq = pairs([unit(w_in2[i]) for i in range(4)])
        U_rk = pairs([unit(w_in2[4 + i]) for i in range(4)])
        U_rv = pairs([unit(w_in2[8 + i]) for i in range(4)])
        U_dec = [unit(decay[:, 0:1024]), unit(decay[:, 1024:2048])]
        U_rg = pairs([unit(w_in2[12 + i]) for i in range(4)])
        U_wo2 = pairs([unit(w_out2[i]) for i in range(8)])
        U_wq = pairs([unit(w_q[i]) for i in range(16)])

        hk = lambda k: one_(hT, k)
        xk = lambda k: one_(xn, k)

        class Squares:
            def __init__(self, cols=None, b=None):
                self.cols, self.wait, self.n, self.b, self.open = cols, [], 0, b, False

            def feed(self, k, t, free=()):
                self.wait.append((k, 0, act(one_(sq, k), hk(k), ACT.Square, t, *free)))
                if self.cols is not None:
                    self.wait.append((k, 1, act(xk(k), hk(k), ACT.Square, t, *free, scale=self.cols(k))))

            def flush(self, below=KD):
                if self.b is None:
                    self.b = bank(7)
                elif not self.open:
                    bank(self.b)
                self.open = True
                total = KD * (1 if self.cols is None else 2)
                for k, j, t in [x for x in self.wait if x[0] < below]:
                    self.n += 1
                    self.t = mm(one_(pb[self.b], j), c_("ones"), one_(sq, k) if j == 0 else xk(k), self.n == 1,
                                self.n == total, t, sig=True, skip=True)
                self.wait = [x for x in self.wait if x[0] >= below]

            def rstd(self, free=()):
                n = T * (1 if self.cols is None else 2)
                t = act(stdt[:, 0:n], pb[self.b][:, 0:n], ACT.Ln, self.t, *free, scale=1.0 / D, bias=c_("eps"))
                readers[self.b] = [t]
                return t

        def inv_root(o, i, *t):
            return act(o, i, ACT.Exp, *t, scale=-0.5)

        table(LNEXP)
        s0 = Squares()
        for k in range(KD):
            s0.feed(k, L_x)
            if k == 0:
                for q in (P, V, A):
                    q.wait(L_cst, L_vec)
        s0.flush()
        t = s0.rstd()
        t_r0 = inv_root(one_(rstd, 0), one_(stdt, 0), t)
        for k in range(KD):
            t = stt(xk(k), hk(k), vc("mix", k), one_(rstd, 0), MUL, MUL, t_r0) if k != 4 else None
            if k == 4:
                t_pos = vcopy(cosT[:, :], posi, L_pos)
                t = stt(xk(k), hk(k), vc("mix", k), one_(rstd, 0), MUL, MUL, t_r0, t_pos)
            split_x(k, xk(k), t)

        lbm, e0, e1, lbd, oml = (small[:, 4 * i:4 * i + 4] for i in range(5))
        sp, su, sp_acc, nsp = (small[:, 20 + 8 * i:24 + 8 * i] for i in range(4))
        cs8 = small[:, 52:60]
        w2_ = small[:, 60:64]
        t = tt(lbm, vc("lb0", 0, 4), vc("lb1", 0, 4), MAX)
        ta = tt(e0, vc("lb0", 0, 4), lbm, SUB, t)
        tb = tt(e1, vc("lb1", 0, 4), lbm, SUB, t)
        t_ = ts(sp, vc("la", 0, 4), -1.0, MUL)
        t_ = tt(su, vc("la", 0, 4), sp, MAX, t_)
        ta = act(e0, e0, ACT.Exp, ta)
        tb = act(e1, e1, ACT.Exp, tb)
        te = act(su, su, ACT.Exp, t_, scale=-1.0)
        t = tt(e1, e0, e1, ADD, ta, tb)
        t = recip(e1, e1, t)
        t = tt(lbd, e0, e1, MUL, t)
        t_lb = ts(oml, lbd, -1.0, MUL, t, s2=1.0, op1=ADD)

        def softplus_table():
            t = ts(sp_acc, su, 2.0, ADD, te)
            t = recip(sp_acc, sp_acc, t)
            t = tt(su, su, sp_acc, MUL, t)
            t = tt(w2_, su, su, MUL, t)
            t = ts(sp_acc, w2_, 1.0 / 17, MUL, t, s2=1.0 / 15, op1=ADD)
            for n in (13, 11, 9, 7, 5, 3, 1):
                t = tt(sp_acc, sp_acc, w2_, MUL, t)
                t = ts(sp_acc, sp_acc, 1.0 / n, ADD, t)
            t = tt(sp_acc, sp_acc, su, MUL, t)
            t = ts(sp, sp, 0.0, MAX, t)
            t = stt(sp, sp_acc, 2.0, sp, MUL, ADD, t)
            return ts(nsp, sp, -LRU_C, MUL, t)

        def rope_tables():
            ang, kk_, rr_ = cosT[:, :], one_(stdt, 0), one_(stdt, 1)
            MAGIC = 12582912.0
            t = ts(ang, ang, c_("invf"), MUL, t_pos, t_r0)
            t = ts(kk_, ang, 1.0 / (2 * math.pi), MUL, t, s2=MAGIC, op1=ADD)
            t = ts(kk_, kk_, -MAGIC, ADD, t)
            c1 = 6.28125
            c2 = float(np.float32(round((2 * math.pi - c1) * 2 ** 21) / 2 ** 21))
            c3 = 2 * math.pi - c1 - c2
            for cc in (c1, c2, c3):
                t = stt(ang, kk_, -cc, ang, MUL, ADD, t)
            PI_ = 3.1415925
            t = ts(ang, ang, PI_, MIN, t, s2=-PI_, op1=MAX)
            t1 = act(sinT[:, :], ang, ACT.Sin, t)
            t2 = act(rr_, ang, ACT.Sin, t, scale=0.5)
            t = tt(rr_, rr_, rr_, MUL, t2)
            return [t1, ts(cosT[:, :], rr_, -2.0, MUL, t, t1, s2=1.0, op1=ADD)]

        sf, ff, kk, lf, bb, eb, kdec, qs, qdec, vtok, kstT, scT = (blk(i) for i in range(12))
        Sst = arena[:, 12 * 1024:14 * 1024]
        lx, xc, lg, gs = xn[:, 0:1024], xn[:, 1024:2048], bb, qs
        t_X = [*X.th.values(), *X.tl.values()]

        table(SIGM)
        t_z = V.do(lambda e: e.memset(scT, 0.0))
        t_sf, t_f = [], []
        for i in range(2):
            b, tk = gemm(U_f[2 * i:2 * i + 2])
            t = act(half(sf, i), pb[b][:, :], ACT.Sigmoid, tk)
            readers[b] = [t]
            t_sf.append(t)
            for h in (2 * i, 2 * i + 1):
                t_f.append(ts(one_(ff, h), one_(sf, h), oml[:, h:h + 1], MUL, t, t_lb, s2=lbd[:, h:h + 1], op1=ADD))
        t_sp = softplus_table()
        t_k = ts(kk, ff, -1.0, MUL, *t_f, s2=1.0, op1=ADD)
        t_qs = []
        for i in range(2):
            b, tk = gemm(U_qq[2 * i:2 * i + 2])
            t = act(half(qs, i), pb[b][:, :], ACT.Sigmoid, tk)
            t = tt(half(qs, i), pb[b][:, :], half(qs, i), MUL, t)
            readers[b] = [t]
            t_qs.append(t)
            if i == 0:
                t_cs = act(cs8, vc("c", 0, 8), ACT.Sigmoid)
                t_c = tt(cs8, cs8, vc("c", 0, 8), MUL, t_cs)
        table(LNEXP)
        t_lf = act(lf, ff, ACT.Ln, *t_f)
        t = V.do(lambda e: e.memset(sq[:, 0:1024], 1.0), s0.t)
        t = V.do(lambda e: e.memset(sq[:, 0:1024:CH], 0.0), t)
        t_b = V.do(lambda e: e.tensor_tensor_scan(bb, sq[:, 0:1024], lf, 0.0, MUL, ADD), t, t_lf)
        bl = v3(bb, CH)[:, :, CH - 1:CH].broadcast_to([128, 32, CH])
        t_d = tt(v3(sf, CH), bl, v3(bb, CH), SUB, t_b, *t_f)
        t_eb = act(eb, bb, ACT.Exp, t_b)
        t_enb = act(kdec, bb, ACT.Exp, t_b, scale=-1.0)
        t_ed = act(sf, sf, ACT.Exp, t_d)
        t_kd = tt(kdec, kk, kdec, MUL, t_enb, t_k)
        t_ks = tt(sf, kk, sf, MUL, t_ed, t_k)
        t_qd = tt(qdec, qs, eb, MUL, t_eb, *t_qs)
        t_xc = []
        for i in range(2):
            b, tk = gemm(U_lx[2 * i:2 * i + 2])
            t = act(half(lx, i), pb[b][:, :], ACT.Copy, tk, *t_X)
            readers[b] = [t]
            for j in (2 * i, 2 * i + 1):
                tj = ts(one_(xc, j), one_(lx, j), vc("conv", 12 + j), MUL, t, *t_X, s2=vc("convb", j), op1=ADD)
                for tap in (2, 1, 0):
                    s = 3 - tap
                    tj = stt(xc[:, j * T + s:(j + 1) * T], lx[:, j * T:(j + 1) * T - s], vc("conv", tap * 4 + j),
                             xc[:, j * T + s:(j + 1) * T], MUL, ADD, tj)
                t_xc.append(tj)
        t_kT = []
        for tile in range(2):
            b = bank(4 + tile)
            for h in range(4):
                fn = lambda e, o=pb[b][:, h * 128:(h + 1) * 128], i=sf[:, h * T + tile * 128:h * T + tile * 128 + 128]: \
                    e.transpose(o, i, c_("ident"))
                tk = P.do(fn, t_ks)
            t = act(half(kstT, tile), pb[b][:, :], ACT.Copy, tk)
            readers[b] = [t]
            t_kT.append(t)
        t_sc = []
        hgm = c_("hgm").bitcast(U32).unsqueeze(1).broadcast_to([128, 4, 128])
        for tile in range(2):
            b = bank(6 + tile)
            for h in range(4):
                s = slice(h * T + tile * 128, h * T + tile * 128 + 128)
                tk = mm(pb[b][:, h * 128:(h + 1) * 128], kdec[:, s], qdec[:, s], True, True, t_kd, t_qd, sig=True)
            t = V.do(lambda e, o=v3(half(scT, tile), 128), i=v3(pb[b][:, :], 128): e.copy_predicated(o, hgm, i), tk, t_z)
            readers[b] = [t]
            t_sc.append(t)
        t_v = []
        bs, tk = gemm_tok(U_i)
        for tile in range(2):
            t = act(half(vtok, tile), pb[bs[tile]][:, :], ACT.Copy, tk)
            readers[bs[tile]] = [t]
            t_v.append(t)
        for hp in range(2):
            b = bank(6 + hp)
            for hh in range(2):
                h = 2 * hp + hh
                for tile in range(2):
                    mm(pb[b][:, hh * T + tile * 128:hh * T + tile * 128 + 128],
                       vtok[:, tile * 512 + h * 128:tile * 512 + h * 128 + 128],
                       scT[:, tile * 512 + h * 128:tile * 512 + h * 128 + 128], hh == 0 and tile == 0, False,
                       t_sc[tile], t_v[tile], skip=True)
        t_S, t_in = [None] * NCH, [None] * NCH
        NS = 4

        def Sof(c):
            return Sst[:, (c % NS) * 512:(c % NS + 1) * 512]

        def state_step(c):
            b = bank(4 + c % 2)
            tile, r = c // 4, 32 * (c % 4)
            for h in range(4):
                tk = mm(pb[b][:, h * 128:(h + 1) * 128], kstT[r:r + 32, tile * 512 + h * 128:tile * 512 + h * 128 + 128],
                        vtok[r:r + 32, tile * 512 + h * 128:tile * 512 + h * 128 + 128], True, True,
                        t_kT[tile], t_v[tile], sig=h == 3)
            fr = [t_in[c + 1 - NS]] if c + 1 - NS >= 1 else []
            if c == 0:
                t = vcopy(Sof(1), pb[b][:, :], tk)
            else:
                for h in range(4):
                    hs = slice(h * 128, (h + 1) * 128)
                    t = stt(Sof(c + 1)[:, hs], Sof(c)[:, hs], eb[:, h * T + c * CH + CH - 1:h * T + c * CH + CH],
                            pb[b][:, hs], MUL, ADD, tk, t_S[c], t_eb, *fr)
            readers[b] = [t]
            t_S[c + 1] = t

        def inter_step(c):
            for h in range(4):
                tk = mm(pb[6 + h // 2][:, (h % 2) * T + c * CH:(h % 2) * T + (c + 1) * CH],
                        Sof(c)[:, h * 128:(h + 1) * 128], qdec[:, h * T + c * CH:h * T + (c + 1) * CH],
                        False, c == NCH - 1, t_S[c], sig=h == 3, skip=True)
            t_in[c] = tk

        def lru_gates():
            t_r, t_ig = [], []
            for gi, (dst, bias, lst) in enumerate(((ff, "ba", t_r), (lf, "bx", t_ig))):
                for i in range(2):
                    b = bank()
                    for jj in range(2):
                        j = 2 * i + jj
                        tk = mm(one_(pb[b], jj), slot(U_lw)[:, (gi * 4 + j) * 128:(gi * 4 + j + 1) * 128],
                                one_(xc, j), True, True, landed(U_lw), t_xc[j], sig=True)
                    for jj in range(2):
                        j = 2 * i + jj
                        t = act(one_(dst, j), one_(pb[b], jj), ACT.Sigmoid, tk, t_k, t_lf, t_b, bias=vc(bias, j))
                        lst.append(t)
                    readers[b] = [t]
            freed[U_lw] = [tk]
            return t_r, t_ig

        table(SIGM)
        t_r, t_ig = lru_gates()
        state_step(0)
        la_, th_, a_, ig_ = kk, lx, ff, lf
        t_la = [ts(one_(la_, j), one_(ff, j), nsp[:, j:j + 1], MUL, t_r[j], t_sp, t_kd, t_ks) for j in range(4)]
        t_th = act(th_, la_, ACT.Tanh, *t_la, *t_xc, scale=-1.0)
        t_i = tt(ig_, ig_, xc, MUL, *t_ig)
        t_lg, t_gs = [], []
        gx = sq[:, 1024:2048]
        for i in range(2):
            b, tk = gemm(U_lg[2 * i:2 * i + 2])
            t = act(half(lg, i), pb[b][:, :], ACT.Copy, tk, t_enb, t_eb, t_d)
            readers[b] = [t]
            g_, x_ = half(gx, i), half(lg, i)
            t = tt(g_, x_, x_, MUL, t)
            t = ts(g_, g_, 0.044715, MUL, t, s2=1.0, op1=ADD)
            t = tt(g_, g_, x_, MUL, t)
            t = act(g_, g_, ACT.Tanh, t, scale=math.sqrt(2.0 / math.pi))
            t = stt(g_, g_, 1.0, x_, ADD, MUL, t)
            t_lg.append(ts(g_, g_, 0.5, MUL, t))
            state_step(1 + 2 * i)
            inter_step(1 + 2 * i)
            state_step(2 + 2 * i)
            inter_step(2 + 2 * i)
        for i in range(2):
            b, tk = gemm(U_g[2 * i:2 * i + 2])
            t = act(half(gs, i), pb[b][:, :], ACT.Sigmoid, tk, t_qd)
            t = tt(half(gs, i), pb[b][:, :], half(gs, i), MUL, t)
            readers[b] = [t]
            t_gs.append(t)
            if i == 0:
                state_step(5)
                inter_step(5)
                state_step(6)
                inter_step(6)
                table(LNEXP)
                t_a = act(a_, la_, ACT.Exp, *t_la)
                t = tt(la_, a_, a_, MUL, t_a, t_th)
                t = stt(la_, la_, 1.0, th_, ADD, MUL, t)
                t = act(la_, la_, ACT.Sqrt, t)
                t_bi = tt(la_, la_, ig_, MUL, t, t_i)
                t = V.do(lambda e: e.memset(a_[:, 0:1024:T], 0.0), t_bi)
                t_h = V.do(lambda e: e.tensor_tensor_scan(th_, a_, la_, 0.0, MUL, ADD), t)
                t_y = tt(th_, th_, gx, MUL, t_h, *t_lg)
                table(SIGM)
        t_win = tk
        inter_step(7)
        M = Halves(X.hi, X.lo)
        for k in range(4, 8):
            split_x(k, one_(th_, k - 4), t_y, M, free=(t_win,))
        table(LNEXP)
        tq, tm = [], []
        for hp in range(2):
            tq.append(act(half(sq, hp), pb[6 + hp][:, :], ACT.Square, t_in[NCH - 1], t_b))
        for hp in range(2):
            b = bank(4 + hp)
            tk = mm(pb[b][:, :], c_("ones"), half(sq, hp), True, True, tq[hp], sig=True)
            t = act(half(stdt, 0), pb[b][:, :], ACT.Ln, tk, *tm[-1:], scale=1.0 / 128, bias=c_("eps"))
            readers[b] = [t]
            t = inv_root(half(rstd, 0), half(stdt, 0), t, *tm[-1:])
            t = stt(half(eb, hp), pb[6 + hp][:, :], vc("hgn"), half(rstd, 0), MUL, MUL, t, t_in[NCH - 1], tq[hp], *t_S[1:])
            readers[6 + hp] = [t]
            tm.append(t)
            t = tt(half(eb, hp), half(eb, hp), half(gs, hp), MUL, t, t_gs[hp])
            for k in (2 * hp, 2 * hp + 1):
                split_x(k, one_(eb, k), t, M, free=(t_win,))

        def residual(us, h, first, squares, gate=None, free=()):
            rest = [k for k in range(KD) if k not in first]
            bs = []
            for i in range(4):
                u2 = us[2 * i:2 * i + 2]
                take(u2)
                bs.append(bank())
                for j, u in enumerate(u2):
                    tk = products(one_(pb[bs[i]], j), u, kc, [*first, *rest], h, same, True, True, True)
                    used(u, tk)
                    if j == 1:
                        for jj in range(2):
                            k = 2 * i + jj
                            if gate is None:
                                tv = tt(hk(k), hk(k), one_(pb[bs[i]], jj), ADD, tk)
                            else:
                                tv = stt(hk(k), one_(pb[bs[i]], jj), gate(k), hk(k), MUL, ADD, tk)
                            squares.feed(k, tv, free)
                        readers[bs[i]] = [tv]
                if i >= 1:
                    squares.flush(2 * i)
            squares.flush()
            return tk

        def normed(squares, scale, shift, dst, t, t_free, h=X):
            for k in range(KD):
                tk = stt(dst(k), hk(k), scale(k), t[0], MUL, MUL, t[1], *t_free)
                if shift is not None:
                    tk = ts(dst(k), dst(k), shift(k), ADD, tk)
                split_x(k, dst(k), tk, h, free=t_free)

        X.th, X.tl = {}, {}
        s1 = Squares()
        tp = residual(U_wo, M, [4, 5, 6, 7], s1, free=(tm[-1],))
        t = s1.rstd()
        t = inv_root(one_(rstd, 0), one_(stdt, 0), t)
        normed(s1, lambda k: vc("ffn", k), None, xk, (one_(rstd, 0), t), (tp, t_y))

        accm = arena[:, 0:6144]
        sgm = [arena[:, 6 * 1024 + i * T:6 * 1024 + (i + 1) * T] for i in range(4)]
        atk = Halves(lambda j: one_(ahi, j), lambda j: one_(alo, j))
        table(SIGM)
        t_rope = rope_tables()
        table(SIGM)
        ringset[0] = [0, 1, 2]
        for b in range(4, 8):
            bank(b)
        t_dn = [None] * NF

        def ada_part(n):
            k, c = n // 6, n % 6
            o, u = accm[:, c * 1024:(c + 1) * 1024], U_ada[n]
            if k == 0:
                t = ts(o, slot(u), cs8[:, 0:1], MUL, landed(u), t_c, *tm)
            else:
                t = stt(o, slot(u), cs8[:, k:k + 1], o, MUL, ADD, landed(u), t_ac[c])
            t_ac[c] = t
            freed[u] = [t]

        t_ac = {}
        s2 = Squares(lambda k: vc("fin", k), b=0)
        for j in range(NF + 2):
            if j < NF:
                b, tk = gemm([U_gate[j], U_up[j]])
                s = sgm[j % 4]
                fr = [atk.th[j - 4], atk.tl[j - 4]] if j >= 4 else []
                t = act(s, one_(pb[b], 0), ACT.Sigmoid, tk, *fr, *t_ac.values() if j < 4 else ())
                t = tt(s, one_(pb[b], 0), s, MUL, t)
                t = tt(s, s, one_(pb[b], 1), MUL, t)
                readers[b] = [t]
                split_x(j, s, t, atk, slot_k=j % 4, free=[t_dn[j - 4]] if j >= 4 else [])
            for n in ada_at[j]:
                ada_part(n)
            if 2 <= j < NF:
                k = j - 2
                take([U_dn[k]])
                for n in range(8):
                    tk = products(one_(pb[4 + n // 2], n % 2), U_dn[k], lambda _, n=n: kc(n), [k], atk, lambda k: k % 4,
                                  k == 0 and n % 2 == 0, False, n == 7, skip=True)
                used(U_dn[k], tk)
                t_dn[k] = tk
        t_ffn = t
        b = bank(3)
        for n in range(48):
            t_ada = mm(pb[b][:, n:n + 1], accm[:, n * 128:(n + 1) * 128], c_("ones")[:, 0:1], True, True, *t_ac.values(),
                       sig=n == 47)
        mod = small[:, 64:112]
        t_mod = tt(mod, pb[b][:, 0:48], vc("adab", 0, 48), ADD, t_ada)
        readers[b] = [t_mod]
        g1s, g2s = small[:, 112:120], small[:, 120:128]
        t1 = stt(g1s, mod[:, 8:16], 1.0, vc("n1", 0, 8), ADD, MUL, t_mod)
        t1 = tt(g1s, g1s, vc("fin", 0, 8), MUL, t1)
        t2 = stt(g2s, mod[:, 32:40], 1.0, vc("n2", 0, 8), ADD, MUL, t_mod)
        t_mods = [t1, t2, t_mod]
        table(LNEXP)
        take(U_dn[NF - 2:])
        for i in range(4):
            for n in (2 * i, 2 * i + 1):
                for k in (NF - 2, NF - 1):
                    tk = products(one_(pb[4 + i], n % 2), U_dn[k], lambda _, n=n: kc(n), [k], atk, lambda k: k % 4,
                                  False, k == NF - 1, True, skip=True)
            for n in (2 * i, 2 * i + 1):
                tv = tt(hk(n), hk(n), one_(pb[4 + i], n % 2), ADD, tk)
                s2.feed(n, tv, (*X.th.values(), *X.tl.values()))
            readers[4 + i] = [tv]
        for u in U_dn[NF - 2:]:
            used(u, tk)
        s2.flush()
        ringset[0] = [0, 1, 2, 3]
        t_gu = tk
        sub = [subk_sb[:, 0:1024], subk_sb[:, 1024:2048]]
        for i in range(2):
            A.quiet(lambda e, i=i: e.dma_start(sub[i], subk[:, i * 1024:(i + 1) * 1024]).then_inc(s_ld[4], 16), tk)
        L_sub = s_ld[4], 32
        t = s2.rstd()
        r1, r2 = one_(rstd, 0), one_(rstd, 1)
        t_r1 = inv_root(r1, one_(stdt, 0), t)
        t = act(one_(stdt, 1), pb[s2.b][:, T:2 * T], ACT.Copy, t)
        readers[s2.b] = [t]
        t = tt(one_(stdt, 1), one_(stdt, 1), r1, MUL, t, t_r1)
        t = tt(one_(stdt, 1), one_(stdt, 1), r1, MUL, t)
        t = act(r2, one_(stdt, 1), ACT.Ln, t, scale=1.0 / D, bias=c_("eps"))
        t = inv_root(r2, r2, t)
        t_rr = tt(r2, r1, r2, MUL, t)
        normed(s2, lambda k: g1s[:, k:k + 1], lambda k: mod[:, k:k + 1], xk, (r2, t_rr), (*t_mods, t_gu, s2.t))
        t_X = [*X.th.values(), *X.tl.values()]
        t_x1 = [stt(hk(k), hk(k), vc("fin", k), r1, MUL, MUL, *t_X) for k in range(KD)]

        rq2, rk2, sbq, sbk, rv, sv, rgs = (blk(i) for i in range(7))
        scR = [arena[:, 7 * 1024 + i * 384:7 * 1024 + (i + 1) * 384] for i in range(4)]
        w9 = 9 * 1024 - 512
        az, be, st = ([arena[:, w9 + (3 * a + i) * 384:w9 + (3 * a + i + 1) * 384] for i in range(3)] for a in range(3))
        raw, tmp, yr, ys = sq[:, 0:1024], sq[:, 1024:2048], xn[:, 0:1024], xn[:, 1024:2048]
        cb = cosT[:, :].unsqueeze(1).broadcast_to([128, 2, T])
        sb_ = sinT[:, :].unsqueeze(1).broadcast_to([128, 2, T])
        t_tmp = {0: s2.t, 1: s2.t}
        t_raw = {0: s2.t, 1: s2.t}

        def rope(us, dst):
            done = []
            for i in range(2):
                b, tk = gemm(us[2 * i:2 * i + 2])
                t = act(half(raw, i), pb[b][:, :], ACT.Copy, tk, t_raw[i])
                readers[b] = [t]
                b2 = bank()
                tk = mm(pb[b2][:, :], c_("rot"), half(raw, i), True, True, t, sig=True)
                ta = tt(v3(half(dst, i), T), v3(half(raw, i), T), cb, MUL, t, *t_rope, *t_ac.values())
                t = tt(v3(half(raw, i), T), v3(pb[b2][:, :], T), sb_, MUL, tk, ta)
                readers[b2] = [t]
                t_raw[i] = tt(half(dst, i), half(dst, i), half(raw, i), ADD, t)
                done.append(t_raw[i])
                hooks()
            return done

        def group_rms(src, gain, i, dst, *t):
            tq = act(half(tmp, i), src, ACT.Square, t_tmp[i], *t)
            b = bank()
            tk = mm(pb[b][:, :], c_("bd64"), half(tmp, i), True, True, tq, sig=True)
            ta = act(half(tmp, i), pb[b][:, :], ACT.Ln, tk, bias=c_("eps"))
            readers[b] = [ta]
            tr = inv_root(half(tmp, i), half(tmp, i), ta)
            t_tmp[i] = stt(dst, src, gain, half(tmp, i), MUL, MUL, tr)
            return t_tmp[i]

        steps = []

        def hooks(n=1):
            for _ in range(n):
                if steps:
                    steps.pop(0)()

        def head_scores(kT, qT, h, t):
            r, j = 64 * (h % 2), h // 2
            b = bank()
            mm(pb[b][:, 0:T], kT[r:r + 64, j * T:j * T + 128], qT[r:r + 64, j * T:(j + 1) * T], True, True, *t)
            tk = mm(pb[b][:, T:T + 128], kT[r:r + 64, j * T + 128:(j + 1) * T], qT[r:r + 64, j * T + 128:(j + 1) * T],
                    True, True, sig=True)
            return b, tk

        def head_out(w, v, h, b, t):
            r, o = 64 * (h % 2), (h // 2 % 2) * T
            mm(pb[b][r:r + 64, o:o + T], v[:, h * 64:(h + 1) * 64], w[:, 0:T], True, False, *t, skip=True)
            return mm(pb[b][r:r + 64, o + 128:o + T], v[:, 512 + h * 64:512 + (h + 1) * 64], w[:, T:T + 128],
                      False, True, sig=True, skip=True)

        def normed_heads(us, dst, gain):
            done = []
            for i in range(2):
                b, tk = gemm(us[2 * i:2 * i + 2])
                t = act(half(dst, i), pb[b][:, :], ACT.Copy, tk, *t_ac.values())
                readers[b] = [t]
                done.append(t)
            return [group_rms(half(dst, i), gain, i, half(dst, i), done[i]) for i in range(2)]

        def token_major(us, dst):
            done = []
            bs, tk = gemm_tok(us)
            for tile in range(2):
                t = act(half(dst, tile), pb[bs[tile]][:, :], ACT.Copy, tk, *t_ac.values())
                readers[bs[tile]] = [t]
                done.append(t)
            return done

        t_sq = normed_heads(U_sq, sbq, vc("sbq"))
        t_sk = normed_heads(U_sk, sbk, vc("sbk"))
        t_sv = token_major(U_sv, sv)

        sbm = c_("sbm").unsqueeze(1).broadcast_to([128, 2, 128])

        def diag(ap):
            return bass.AP(ap.tensor, ap.offset, [ap.ap[0], [256, 2], [1, 128]])

        t_be, t_st, t_w, t_ys, t_cum = {}, {}, {}, {}, {}

        def sb_logits(h):
            n = h % 3
            b, tk = head_scores(sbk, sbq, h, [*t_sq, *t_sk])
            t_abs = act(az[n], pb[b][:, 0:384], ACT.Abs, tk, *([t_ys[h - 3]] if h >= 3 else [s2.t]), scale=0.125)
            t = act(az[n], az[n], ACT.Exp, t_abs, scale=-1.0)
            t = act(az[n], az[n], ACT.Ln, t, bias=c_("one"))
            tb = ts(be[n], pb[b][:, 0:384], 0.125, MUL, t_abs, *([t_w[h - 3]] if h >= 3 else []), s2=0.0, op1=MIN)
            tb = tt(be[n], be[n], az[n], SUB, tb, t)
            t = stt(st[n], pb[b][:, 0:384], -0.125, be[n], MUL, ADD, tb, *([t_cum[h - 3]] if h >= 3 else []))
            readers[b] = [t]
            t_be[h] = tb
            t_st[h] = tt(diag(st[n]), diag(st[n]), sbm, MUL, t)

        def sb_weights(h):
            n = h % 3
            b = bank()
            mm(pb[b][:, 0:384], c_("tri"), st[n], True, False, t_st[h], skip=True)
            tk = mm(pb[b][:, 128:256], c_("ones"), st[n][:, 256:384], False, True, sig=True, skip=True)
            t_cum[h] = tk
            t = tt(be[n], be[n], pb[b][:, 0:384], ADD, tk, t_be[h])
            readers[b] = [t]
            t = act(az[n], be[n], ACT.Exp, t)
            t_w[h] = tt(diag(az[n]), diag(az[n]), sbm, MUL, t)

        def sb_out(h):
            if h % 4 == 0:
                bank(6 + h // 4)
            t_ys[h] = head_out(az[h % 3], sv, h, 6 + h // 4, [t_w[h], *t_sv])

        def sb_step(i):
            if i < 8:
                sb_logits(i)
            if 1 <= i <= 8:
                sb_weights(i - 1)
            if 2 <= i:
                sb_out(i - 2)

        M = Halves(X.hi, X.lo)
        t_sbn = {}

        def sb_norm(i):
            t = act(half(ys, i), pb[6 + i][:, :], ACT.Copy, t_ys[4 * i + 3], *t_X)
            readers[6 + i] = [t]
            t_sbn[i] = group_rms(half(ys, i), vc("sbo"), i, half(ys, i), t)

        steps += [lambda i=i: sb_step(i) for i in range(10)]
        steps += [lambda i=i: sb_norm(i) for i in range(2)]
        hooks()
        t_rq = rope(U_rq, rq2)
        hooks()
        t_rk = rope(U_rk, rk2)
        hooks(2)
        t_rv = token_major(U_rv, rv)
        hooks(2)

        t_scR, t_yr = {}, {}

        def ret_scores(h):
            b, tk = head_scores(rk2, rq2, h, [*t_rq, *t_rk])
            dec = slot(U_dec[h // 4])[:, (h % 4) * T:(h % 4 + 1) * T]
            w = scR[h % 4]
            fr = [t_yr[h - 4]] if h >= 4 else []
            tt(w[:, 0:T], pb[b][:, 0:T], dec, MUL, tk, landed(U_dec[h // 4]), *fr)
            t = tt(w[:, T:T + 128], pb[b][:, T:T + 128], dec[:, 0:128], MUL)
            readers[b] = [t]
            t_scR[h] = t
            freed[U_dec[h // 4]] = [t]

        def ret_out(h):
            if h % 4 == 0:
                bank(4 + h // 4)
            t_yr[h] = head_out(scR[h % 4], rv, h, 4 + h // 4, [t_scR[h], *t_rv])

        t_rg = []
        t_yc = {}

        def ret_mean(i):
            t = act(half(yr, i), pb[4 + i][:, :], ACT.Copy, t_yr[4 * i + 3], *t_X)
            readers[4 + i] = [t]
            b = bank()
            tk = mm(pb[b][:, :], c_("bd64"), half(yr, i), True, True, t, sig=True)
            t = tt(half(yr, i), half(yr, i), pb[b][:, :], SUB, tk)
            readers[b] = [t]
            t_yc[i] = t

        for i in range(2):
            for h in range(4 * i, 4 * i + 4):
                ret_scores(h)
                if h:
                    ret_out(h - 1)
                if h == 5:
                    ret_mean(0)
            b, tk = gemm(U_rg[2 * i:2 * i + 2])
            hooks()
            if i == 1:
                ret_out(7)
                ret_mean(1)
                table(SIGM)
                for j, (bb_, tt_) in enumerate(((b0, tk0), (b, tk))):
                    t = act(half(rgs, j), pb[bb_][:, :], ACT.Sigmoid, tt_)
                    t = tt(half(rgs, j), pb[bb_][:, :], half(rgs, j), MUL, t)
                    readers[bb_] = [t]
                    t_rg.append(t)
                table(LNEXP)
            else:
                b0, tk0 = b, tk
                readers[b0] = []
                ringset[0] = [x for x in range(4) if x != b0]
        ringset[0] = [0, 1, 2, 3]
        hooks(12)
        t_win2 = tk
        for i in range(2):
            for k in (2 * i, 2 * i + 1):
                split_x(4 + k, one_(ys, k), t_sbn[i], M, free=(t_win2,))
        for i in range(2):
            tq = act(half(tmp, i), half(yr, i), ACT.Square, t_yc[i], t_tmp[i])
            b = bank()
            tk = mm(pb[b][:, :], c_("bd64"), half(tmp, i), True, True, tq, sig=True)
            ta = act(half(tmp, i), pb[b][:, :], ACT.Ln, tk, bias=c_("eps"))
            readers[b] = [ta]
            tr = inv_root(half(tmp, i), half(tmp, i), ta)
            for k in (2 * i, 2 * i + 1):
                t = stt(one_(yr, k), one_(yr, k), vc("retg", k), one_(tmp, k), MUL, MUL, tr)
                t = tt(one_(yr, k), one_(yr, k), one_(rgs, k), MUL, t, t_rg[i])
                split_x(k, one_(yr, k), t, M, free=(t_win2,))
            t_tmp[i] = t
        s3 = Squares()
        tp = residual(U_wo2, M, [4, 5, 6, 7], s3, gate=lambda k: mod[:, 16 + k:17 + k],
                      free=(*t_x1, *t_tmp.values(), *t_raw.values()))
        t = s3.rstd()
        t = inv_root(one_(rstd, 0), one_(stdt, 0), t)
        X = Halves(X.hi, X.lo)
        normed(s3, lambda k: g2s[:, k:k + 1], lambda k: mod[:, 24 + k:25 + k], xk, (one_(rstd, 0), t),
               (tp, s3.t, *M.tl.values(), *M.th.values()), h=X)
        t_X = [*X.th.values(), *X.tl.values()]

        SC = [blk(0, 2048), blk(2, 2048)]
        h2t, x2t, g2b = [blk(4), blk(5)], [blk(6), blk(7)], blk(8)
        pk = arena[:, 9 * 1024:12 * 1024]
        dgr = [arena[:, 12 * 1024 + i * 128:12 * 1024 + (i + 1) * 128] for i in range(16)]
        qry = [sq[:, 0:512], sq[:, 512:1024]]
        dg = sq[:, 1024:2048]
        f32c = lambda o, n: pk[:, o:o + n]
        tsv, tif, abf, iab = f32c(0, 32), f32c(32, 32), f32c(64, 32), f32c(96, 32)
        bsv, nb, ssum = f32c(128, 16), f32c(144, 1), f32c(145, 1)
        sc2 = f32c(160, 256)
        cand, cand2 = f32c(416, 256), f32c(672, 256)
        eq = f32c(928, 512)
        gts, aa, ae, ex = f32c(1440, 256), f32c(1696, 256), f32c(1952, 256), f32c(2208, 256)

        t_SC = {}
        t_sco = {}

        def query(h):
            b, tk = gemm(U_wq[2 * h:2 * h + 2])
            t = act(qry[h % 2], pb[b][:, :], ACT.Copy, tk, s3.t, *([t_sco[h - 2]] if h >= 2 else []))
            readers[b] = [t]
            b = bank()
            for tile in range(2):
                for p in range(2):
                    c = (2 * h + p) % 8
                    tk = mm(pb[b][:, (2 * tile + p) * 128:(2 * tile + p + 1) * 128],
                            qry[h % 2][:, p * T + tile * 128:p * T + tile * 128 + 128], sub[h // 4][:, c * 128:(c + 1) * 128],
                            True, True, t, L_sub, sig=True)
            t_sco[h] = tk
            for tile in range(2):
                t = act(SC[tile][:, h * 256:(h + 1) * 256], pb[b][:, tile * 256:(tile + 1) * 256], ACT.Copy, tk)
            readers[b] = [t]
            t_SC[h] = t

        def turned(src, dst, t0):
            lst = []
            for tile in range(2):
                for g in range(2):
                    b = bank()
                    for n in range(4):
                        fn = lambda e, o=pb[b][:, n * 128:(n + 1) * 128], \
                            i=src(4 * g + n)[:, tile * 128:(tile + 1) * 128]: e.transpose(o, i, c_("ident"))
                        tk = P.do(fn, *t0)
                    t = act(dst[tile][:, g * 512:(g + 1) * 512], pb[b][:, :], ACT.Copy, tk)
                    readers[b] = [t]
                    lst.append(t)
            return lst

        def gate_rows():
            lst = []
            for g in range(2):
                b = bank()
                for n in range(4):
                    k = 4 * g + n
                    t = ts(dg[:, k * 128:(k + 1) * 128], c_("ident"), mod[:, 40 + k:41 + k], MUL, s3.t)
                    tk = mm(pb[b][:, n * 128:(n + 1) * 128], c_("ones"), dg[:, k * 128:(k + 1) * 128], True, True, t,
                            sig=True)
                t = act(g2b[:, g * 512:(g + 1) * 512], pb[b][:, :], ACT.Copy, tk)
                readers[b] = [t]
                lst.append(t)
            return lst

        def top16(src, tmp_, vals, idx, *t):
            t1 = V.do(lambda e: e.max(vals[:, 0:8], src), *t)
            V.do(lambda e: e.max_index(idx[:, 0:8], vals[:, 0:8], src), t1)
            t1 = V.do(lambda e: e.match_replace(tmp_, vals[:, 0:8], src, NEG), t1)
            t1 = V.do(lambda e: e.max(vals[:, 8:16], tmp_), t1)
            return V.do(lambda e: e.max_index(idx[:, 8:16], vals[:, 8:16], tmp_), t1)

        t_ids, t_gt = {}, {}

        def choose(n):
            tile, h = n // 8, n % 8
            for p in range(2):
                s = SC[tile][:, (2 * h + p) * 128:(2 * h + p + 1) * 128]
                t = top16(s, sc2[:, 0:128], tsv[:, p * 16:p * 16 + 16], tiu[:, p * 16:p * 16 + 16],
                          t_SC[h], (V.sem, V.n))
            tf = vcopy(tif, tiu[:, :], t)
            t = tt(v3(cand, 16), tsv[:, 0:16].unsqueeze(2).broadcast_to([128, 16, 16]),
                   tsv[:, 16:32].unsqueeze(1).broadcast_to([128, 16, 16]), ADD, t)
            exn = ex[:, n * 16:(n + 1) * 16]
            t = top16(cand, cand2, bsv, bcu[:, :], t, *([t_gt[n - 1][0]] if n else []))
            tn = ts(nb, bsv[:, 0:1], -1.0, MUL, t)
            te = act(exn, bsv, ACT.Exp, tn, bias=nb, accum_out=ssum)
            ta = V.do(lambda e: e.tensor_scalar(abu[:, 0:16], bcu[:, :], 4, None, ALU.logical_shift_right), t)
            tb = V.do(lambda e: e.tensor_scalar(abu[:, 16:32], bcu[:, :], 15, None, ALU.bitwise_and), t)
            t = vcopy(abf, abu[:, :], ta, tb)
            t = tt(v3(eq, 16), c_("iota").unsqueeze(1).broadcast_to([128, 32, 16]),
                   abf.unsqueeze(2).broadcast_to([128, 32, 16]), ALU.is_equal, t)
            e4 = eq.rearrange("p (a s m) -> p a s m", a=2, m=16)
            t = tt(e4, e4, tif.rearrange("p (a m) -> p a m", a=2).unsqueeze(2).broadcast_to([128, 2, 16, 16]), MUL, t, tf)
            t = V.do(lambda e: e.tensor_reduce(iab, v3(eq, 16), AX_X, ADD), t)
            t_ids[n] = stt(idsb[:, n * 16:(n + 1) * 16], iab[:, 0:16], 128.0, iab[:, 16:32], MUL, ADD, t)
            tr = recip(ssum, ssum, te)
            t = ts(gts[:, n * 16:(n + 1) * 16], exn, ssum, MUL, tr)
            t_gt[n] = (te, t)

        first_u = len(units) - SLOTS
        slot_free = {u % SLOTS: None for u in range(first_u, len(units))}
        slot_uses = {s: 0 for s in range(SLOTS)}
        nxt = [0]

        def gather(table_, col, tk_ids):
            s = (first_u + nxt[0]) % SLOTS
            if nxt[0] < SLOTS:
                slot_free[s] = freed[first_u + nxt[0]]
            nxt[0] += 1
            o = ring_sb[:, s * 1024:(s + 1) * 1024]
            slot_uses[s] += 1
            G.quiet(lambda e: e.indirect_dma_start(
                o, None, table_, bass.IndirectOffsetOnAxis(ap=idsb[:, col:col + 1], axis=0)).then_inc(s_row[s], 16),
                tk_ids, *slot_free[s])
            slot_free[s] = None
            return s, o, (s_row[s], 16 * slot_uses[s])

        R = 4
        NB = 256 // R
        BPC = 16 // R
        downs = {}
        t_mmu = {}

        def down_rows(i):
            downs[i] = [gather(peer_down, i * R + j, t_ids[i // BPC]) for j in range(R)]

        def down_dots(i):
            tile = i // (NB // 2)
            for j in range(R):
                s, o, tl = downs[i][j]
                col = i * R + j
                t = V.do(lambda e, o=o, col=col, tile=tile: e.tensor_tensor_reduce(
                    o, o, h2t[tile], 1.0, 0.0, MUL, ADD, aa[:, col:col + 1]), tl, *t_h2t)
                slot_free[s] = [t]
            return act(ae[:, i * R:i * R + R], aa[:, i * R:i * R + R], ACT.Gelu, t)

        def weights_of(i, te):
            cols = slice(i * R, i * R + R)
            t = tt(ae[:, cols], ae[:, cols], gts[:, cols], MUL, te, t_gt[i // BPC][1])
            return [act(dgr[col % 16], c_("ident"), ACT.Copy, t, *([t_mmu[col - 16]] if col >= 16 else []),
                        scale=ae[:, col:col + 1]) for col in range(i * R, i * R + R)]

        def up_sums(i, t_dg):
            tile = i // (NB // 2)
            ups = [gather(peer_up, i * R + j, t_ids[i // BPC]) for j in range(R)]
            for j in range(R):
                s, o, tl = ups[j]
                col = i * R + j
                first, last = col % 128 == 0, col % 128 == 127
                if first:
                    bank(4 + 2 * tile)
                    bank(5 + 2 * tile)
                mm(pb[4 + 2 * tile][:, :], dgr[col % 16], o[:, 0:512], first, last, tl, t_dg[j])
                tk = mm(pb[5 + 2 * tile][:, :], dgr[col % 16], o[:, 512:1024], first, last, sig=True)
                t_mmu[col] = tk
                slot_free[s] = [tk]
            return tk

        def experts(i):
            if i + 1 < NB and i + 1 not in downs:
                down_rows(i + 1)
            te = down_dots(i)
            if i % BPC == 1 and i // BPC + 2 < 16:
                choose(i // BPC + 2)
            return up_sums(i, weights_of(i, te))

        t_h2t = None
        for h in range(8):
            query(h)
            if h == 0:
                t_h2t = turned(xk, h2t, t_X)
            if h <= 1:
                choose(h)
            if h == 2:
                down_rows(0)
            if h == 3:
                down_rows(1)
            if h == 6:
                experts(0)
        t_x2t = turned(hk, x2t, [s3.t])
        t_g2 = gate_rows()
        for i in range(1, NB):
            tk = experts(i)
            if i % (NB // 2) == NB // 2 - 1:
                tile = i // (NB // 2)
                for g in range(2):
                    gsl = slice(g * 512, (g + 1) * 512)
                    t = tt(dg[:, 0:512], pb[4 + 2 * tile + g][:, :], g2b[:, gsl], MUL, tk, *t_g2,
                           (V.sem, V.n))
                    t = tt(x2t[tile][:, gsl], x2t[tile][:, gsl], dg[:, 0:512], ADD, t, *t_x2t)
                A.quiet(lambda e, tile=tile: e.dma_start(out[tile * 128:(tile + 1) * 128, :], x2t[tile]).then_inc(s_out, 16), t)

        for u, src in enumerate(units):
            SY.quiet(lambda e, u=u, src=src: e.dma_start(slot(u), src).then_inc(s_slot[u % SLOTS], 16),
                     *(freed[u - SLOTS] if u >= SLOTS else []))
        SY.wait((s_out, 32))

        block = ctx.enter_context(nc.Block())

        @block.sync
        def _(e):
            SY.run(e)

        @block.gpsimd
        def _(e):
            G.run(e)

        @block.scalar
        def _(e):
            A.run(e)

        @block.vector
        def _(e):
            V.run(e)

        @block.tensor
        def _(e):
            P.run(e)


def kernel(**inputs):
    import numpy as _np
    import concourse.bacc as _bacc
    from concourse import mybir as _mybir
    from concourse.bass_utils import run_bass_kernel_spmd as _run

    a = {k: _np.asarray(v) for k, v in inputs.items()}

    def fm(v):
        return v.reshape(-1, 128).T

    def units(w):
        n = w.shape[1] // 128
        return _np.ascontiguousarray(w.reshape(8, 128, n, 128).transpose(2, 1, 0, 3)).reshape(n, 128, 1024)

    def twice(v):
        return _np.concatenate([v.reshape(-1), v.reshape(-1)]).reshape(128, 1)

    vecs = _np.concatenate([
        fm(a["mix_norm_w"]), fm(a["ffn_norm_w"]), fm(a["final_norm_w"]), fm(a["norm1_gain_2"]), fm(a["norm2_gain_2"]),
        fm(a["conv_w"][0]), fm(a["conv_b"]), fm(a["lru_ba"]), fm(a["lru_bx"]), fm(a["lru_a"]),
        fm(a["hg_lb"][0]), fm(a["hg_lb"][1]), fm(a["hg_norm_w"]), fm(a["ret_norm_gain_2"]),
        twice(a["sb_q_gain_2"]), twice(a["sb_k_gain_2"]), twice(a["sb_out_gain_2"]), fm(a["ada_b_2"]), fm(a["c_2"]),
    ], axis=1)
    lw = _np.zeros((128, 8, 128), _np.float32)
    for g, w in enumerate((a["lru_wa"][0], a["lru_wx"][0])):
        for j in range(4):
            lw[0:64, g * 4 + j, 0:64] = w[2 * j]
            lw[64:128, g * 4 + j, 64:128] = w[2 * j + 1]
    cst, dec = shape_constants()
    arrays = {
        "xT": a["x"][0].T.reshape(8, 128, 256).transpose(1, 0, 2).reshape(128, 2048),
        "vecs": vecs, "cst": cst, "decay": dec, "pos": a["positions_2"],
        "w_in": units(a["w_in"][0]), "w_out": units(a["w_out"][0]), "w_gu": units(a["w_gate_up"][0]),
        "w_down": a["w_down"][0].reshape(22, 128, 1024), "ada": a["ada_w_2"][0],
        "w_in2": units(a["w_in_2"][0]), "w_out2": units(a["w_out_2"][0]), "w_q": units(a["peer_w_query_2"][0]),
        "subk": a["peer_sub_keys_2"][0].reshape(16, 128, 128).transpose(2, 0, 1).reshape(128, 2048),
        "lru_w": lw.reshape(128, 1024),
        "peer_down": a["peer_down_2"][0], "peer_up": a["peer_up_2"][0],
    }
    nc = _bacc.Bacc("TRN2", target_bir_lowering=False, num_devices=1)
    feed, args = {}, []
    for name, v in arrays.items():
        v = _np.ascontiguousarray(v)
        feed[f"in_{name}"] = v
        args.append(nc.dram_tensor(f"in_{name}", v.shape, _mybir.dt.from_np(v.dtype), kind="ExternalInput").ap())
    o = nc.dram_tensor("out_0", (256, 1024), _mybir.dt.float32, kind="ExternalOutput").ap()
    build(nc, *args, o)
    r = _run(nc, [feed], core_ids=[0])
    return r.results[0]["out_0"].reshape(1, 256, 1024)
```

```python
import math
from contextlib import ExitStack

import numpy as np

import concourse.bass as bass
from concourse import mybir

ALU = mybir.AluOpType
ACT = mybir.ActivationFunctionType
F32 = mybir.dt.float32
F32R = mybir.dt.float32r
U32 = mybir.dt.uint32
I32 = mybir.dt.int32
AX_X = mybir.AxisListType.X

T = 256
D = 1024
KD = D // 128
FF = 2816
NF = FF // 128
CH = 32
NCH = T // CH
LRU_C = 8.0
EPS = 1e-6
SLOTS = 16
WS = 6
NEXP = 16384
NEG = -3.0e38

VEC = {}
_at = 0
for _name, _n in (("mix", 8), ("ffn", 8), ("fin", 8), ("n1", 8), ("n2", 8), ("conv", 16), ("convb", 4), ("ba", 4),
                  ("bx", 4), ("la", 4), ("lb0", 4), ("lb1", 4), ("hgn", 1), ("retg", 4), ("sbq", 1), ("sbk", 1),
                  ("sbo", 1), ("adab", 48), ("c", 8)):
    VEC[_name] = (_at, _n)
    _at += _n
NVEC = _at

CST = {}
_at = 0
for _name, _n in (("ident", 128), ("rot", 128), ("ones", 128), ("bd64", 128), ("tri", 128), ("sbm", 128),
                  ("hgm", 128), ("iota", 16), ("invf", 1), ("eps", 1), ("eps2", 1), ("one", 1), ("zero", 1)):
    CST[_name] = (_at, _n)
    _at += _n
NCST = _at


def shape_constants():
    c = np.zeros((128, NCST), np.float32)

    def put(name, a):
        s, n = CST[name]
        c[:, s:s + n] = np.asarray(a, np.float32).reshape(128, n)

    p = np.arange(128)
    put("ident", np.eye(128))
    rot = np.zeros((128, 128))
    for m in range(128):
        if m % 64 < 32:
            rot[m + 32, m] = -1.0
        else:
            rot[m - 32, m] = 1.0
    put("rot", rot)
    put("ones", np.ones((128, 128)))
    put("bd64", (p[:, None] // 64 == p[None, :] // 64) / 64.0)
    put("tri", p[:, None] > p[None, :])
    put("sbm", p[:, None] < p[None, :])
    put("hgm", (p[:, None] // CH == p[None, :] // CH) & (p[:, None] <= p[None, :]))
    put("iota", np.tile(np.arange(16), (128, 1)))
    put("invf", np.float32(10000.0) ** (-(p % 32).astype(np.float32) / np.float32(32)))
    put("eps", np.full(128, EPS))
    put("eps2", np.full(128, EPS * EPS))
    put("one", np.ones(128))
    dec = np.zeros((128, 8, T), np.float32)
    rel = np.arange(T)[None, :] - p[:, None]
    for h in range(8):
        lg = np.float32(np.log1p(-(2.0 ** (-5.0 - h))))
        dec[:, h] = np.where(rel >= 0, np.exp(np.float64(lg) * np.maximum(rel, 0)) * 0.125, 0.0)
    return c, dec.reshape(128, 8 * T)


class Queue:

    def __init__(self, sem):
        self.sem, self.n, self.items, self.past = sem, 0, [], {}

    def wait(self, *tickets):
        for sem, v in tickets:
            if self.past.get(sem.num, 0) < v:
                self.past[sem.num] = v
                self.items.append(lambda e, sem=sem, v=v: e.wait_ge(sem, v))

    def quiet(self, fn, *tickets):
        self.wait(*tickets)
        self.items.append(fn)

    def do(self, fn, *tickets):
        self.wait(*tickets)
        self.n += 1
        self.items.append(lambda e: fn(e).then_inc(self.sem, 1))
        return self.sem, self.n

    def run(self, eng):
        for f in self.items:
            f(eng)


def build(nc, xT, vecs, cst, decay, pos, w_in, w_out, w_gu, w_down, ada, w_in2, w_out2, w_q, w_iv, w_sv, w_rv, subk, lru_w,
          peer_down, peer_up, out):
    ctx = ExitStack()
    with ctx:
        def sb(name, n, dt=F32):
            return ctx.enter_context(nc.sbuf_tensor(name, [128, n], dt))

        def sem(name):
            return ctx.enter_context(nc.semaphore(name))

        with nc.sbuf_tensor("ring_lo", [128, SLOTS * 1024], F32R) as ring_lo, \
                nc.sbuf_tensor("skip0", [128, 2 * 1024], F32), \
                nc.sbuf_tensor("more_lo", [128, 12 * 1024], F32R) as more_lo, \
                nc.sbuf_tensor("ahi", [128, 4 * T], F32R) as ahi, nc.sbuf_tensor("alo", [128, 4 * T], F32R) as alo:
            pass
        ring_sb = sb("ring_sb", SLOTS * 1024)
        NBLK = 14
        arena = sb("arena", NBLK * 1024)
        subk_sb = sb("subk_sb", 2048)
        whi = sb("whi", WS * 1024, F32R)
        one_r = sb("one_r", 128, F32R)
        xhi = sb("xhi", 2048, F32R)
        xlo = sb("xlo", 2048, F32R)
        hT = sb("hT", 2048)
        xn = sb("xn", 2048)
        sq = sb("sq", 2048)
        cs = sb("cs", NCST)
        vv = sb("vv", NVEC)
        cosT = sb("cosT", T)
        sinT = sb("sinT", T)
        rstd = sb("rstd", 512)
        stdt = sb("stdt", 512)
        small = sb("small", 256)
        idsb = sb("idsb", 256, U32)
        tiu = sb("tiu", 32, U32)
        bcu = sb("bcu", 16, U32)
        abu = sb("abu", 32, U32)
        pb = [ctx.enter_context(nc.psum_tensor(f"pb{i}", [128, 512], F32)) for i in range(8)]

        def blk(i, n=1024):
            return arena[:, i * 1024:i * 1024 + n]

        def v3(ap, m):
            return ap.rearrange("p (n m) -> p n m", m=m)

        def half(ap, i):
            return ap[:, i * 512:(i + 1) * 512]

        def one_(ap, h):
            return ap[:, h * T:(h + 1) * T]

        def c_(name):
            s, n = CST[name]
            return cs[:, s:s + n]

        def vc(name, j=0, n=1):
            s = VEC[name][0] + j
            return vv[:, s:s + n]

        P = Queue(sem("s_pe"))
        V = Queue(sem("s_dve"))
        A = Queue(sem("s_act"))
        G = Queue(sem("s_pool"))
        SY = Queue(sem("s_sp"))
        s_ld = [sem(f"s_ld{i}") for i in range(5)]
        s_x = [sem(f"s_x{i}") for i in range(4)]
        s_slot = [sem(f"s_slot{i}") for i in range(SLOTS)]
        s_row = [sem(f"s_row{i}") for i in range(SLOTS + 5)]
        s_out = sem("s_out")

        def act(o, i, f, *t, **kw):
            return A.do(lambda e: e.activation(o, i, f, **kw), *t)

        def tt(o, a, b, op, *t):
            return V.do(lambda e: e.tensor_tensor(o, a, b, op), *t)

        def ts(o, a, s1, op0, *t, s2=None, op1=None):
            if op1 is None:
                return V.do(lambda e: e.tensor_scalar(o, a, s1, None, op0), *t)
            return V.do(lambda e: e.tensor_scalar(o, a, s1, s2, op0, op1), *t)

        def stt(o, a, s, b, op0, op1, *t):
            return V.do(lambda e: e.scalar_tensor_tensor(out=o, in0=a, scalar=s, in1=b, op0=op0, op1=op1), *t)

        def vcopy(o, i, *t):
            return V.do(lambda e: e.tensor_copy(o, i), *t)

        def recip(o, i, *t):
            return V.do(lambda e: e.reciprocal(o, i), *t)

        def mm(o, l, r, start, stop, *t, sig=False, skip=False):
            fn = lambda e: e.matmul(o, l, r, start=start, stop=stop, skip_group_check=skip)
            return P.do(fn, *t) if sig else P.quiet(fn, *t)

        def table(name):
            A.quiet(lambda e: e.preload_act_table_set(name))

        MUL, ADD, SUB, MAX, MIN = ALU.mult, ALU.add, ALU.subtract, ALU.max, ALU.min
        LNEXP, SIGM = "natural_log_exp_and_others", "sigmoid_and_others"

        readers = [[] for _ in range(8)]
        turn = [0]
        ringset = [[0, 1, 2, 3]]

        def bank(i=None):
            if i is None:
                i = ringset[0][turn[0] % len(ringset[0])]
                turn[0] += 1
            P.wait(*readers[i])
            readers[i] = []
            return i

        def keep_clock(n):
            b = bank()
            for _ in range(n):
                mm(pb[b][:, 0:128], c_("ones"), c_("ident"), True, True, skip=True)

        units, freed, place, nth, before = [], {}, [], [], []
        last, cyc = {}, [0]

        def unit(src, where=None):
            if where is None:
                where = cyc[0] % SLOTS
                cyc[0] += 1
            u = len(units)
            units.append(src)
            place.append(where)
            before.append(last.get(where))
            nth.append(1 if before[u] is None else nth[before[u]] + 1)
            last[where] = u
            return u

        def slot(u):
            return ring_sb[:, place[u] * 1024:(place[u] + 1) * 1024]

        def landed(u):
            return s_slot[place[u]], 16 * nth[u]

        groups, ngroup, nsplit = [], [0], [0]
        wsp, wfree = {}, [[] for _ in range(WS)]

        def split_unit(u, pool=False):
            s = nsplit[0] % WS
            hi, lo = whi[:, s * 1024:(s + 1) * 1024], ring_lo[:, place[u] * 1024:(place[u] + 1) * 1024]
            th = act(hi, slot(u), ACT.Copy, landed(u), *wfree[s])
            q = V if not pool and (nsplit[0] % 4 == 3 or u in U_wq[8:]) else G
            tl = q.do(lambda e: e.tensor_tensor(lo, slot(u), hi.bitcast(F32), SUB), landed(u), th)
            wsp[u] = (s, hi, lo, th, tl)
            nsplit[0] += 1

        def used(u, tk):
            wfree[wsp[u][0]] = [tk]
            freed[u] = [tk]
            held[0] -= 1

        held = [0]

        def ahead(first=None, n=None, pool=False):
            first = ngroup[0] if first is None else first
            for g in range(first, len(groups) if n is None else first + n):
                new = [u for u in groups[g] if u not in wsp]
                if held[0] + len(new) > WS:
                    break
                for u in new:
                    split_unit(u, pool)
                held[0] += len(new)

        def take(us, more=True):
            assert groups[ngroup[0]] == us
            ngroup[0] += 1
            ahead(ngroup[0] - 1, None if more else 1)

        class Halves:

            def __init__(self, hi, lo):
                self.hi, self.lo, self.th, self.tl = hi, lo, {}, {}

        X = Halves(lambda k: one_(xhi, k), lambda k: one_(xlo, k))

        def split_x(k, src, t, h=X, slot_k=None, free=()):
            j = k if slot_k is None else slot_k
            h.th[k] = act(h.hi(j), src, ACT.Copy, t, *free)
            h.tl[k] = V.do(lambda e: e.tensor_tensor(h.lo(j), src, h.hi(j).bitcast(F32), SUB), h.th[k], t, *free)

        def products(o, u, c, ks, h, hk, start, stop, sig, skip=False):
            s, hi, lo, th, tl = wsp[u]
            P.wait(th)
            for i, k in enumerate(ks):
                mm(o, hi[:, c(k)], h.hi(hk(k)), start and i == 0, False, h.th[k], skip=skip)
                mm(o, hi[:, c(k)], h.lo(hk(k)), False, False, h.tl[k], skip=skip)
            for i, k in enumerate(ks):
                last = i == len(ks) - 1
                tk = mm(o, lo[:, c(k)], h.hi(hk(k)), False, stop and last, tl, sig=sig and last, skip=skip)
            return tk

        kc = lambda k: slice(k * 128, (k + 1) * 128)
        same = lambda k: k

        steps = []

        def hooks(n=1):
            for _ in range(n):
                if steps:
                    steps.pop(0)()

        def gemm(us, fresh=False, mid=None):
            take(us)
            b = bank()
            if fresh:
                for k in range(KD):
                    for i, u in enumerate(us):
                        tk = products(one_(pb[b], i), u, kc, [k], X, same, k == 0 and i == 0, k == KD - 1, True, skip=True)
                for u in us:
                    used(u, tk)
                return b, tk
            for i, u in enumerate(us):
                tk = products(one_(pb[b], i), u, kc, range(KD), X, same, True, True, True)
                used(u, tk)
                if i == 0:
                    (mid or hooks)()
            return b, tk

        def gemm_tok(us4):
            bs = [bank(), bank()]
            for p in range(2):
                us = us4[2 * p:2 * p + 2]
                if p:
                    hooks()
                take(us)
                for i, u in enumerate(us):
                    s, hi, lo, th, tl = wsp[u]
                    P.wait(th)
                    for kk in range(2):
                        k, cols = 4 * p + 2 * i + kk, slice(kk * 512, (kk + 1) * 512)
                        for tile in range(2):
                            o, tok = pb[bs[tile]][:, :], slice(tile * 128, (tile + 1) * 128)
                            mm(o, X.hi(k)[:, tok], hi[:, cols], k == 0, False, X.th[k])
                            mm(o, X.lo(k)[:, tok], hi[:, cols], False, False, X.tl[k])
                            tk = mm(o, X.hi(k)[:, tok], lo[:, cols], False, k == KD - 1, tl, sig=True)
                    used(u, tk)
            return bs, tk

        for i in range(4):
            SY.quiet(lambda e, i=i: e.dma_start(half(hT, i), half(xT, i)).then_inc(s_x[i], 16))
        SY.quiet(lambda e: e.dma_start(cs[:, :], cst).then_inc(s_ld[0], 16))
        SY.quiet(lambda e: e.dma_start(vv[:, :], vecs).then_inc(s_ld[3], 16))
        posi = xn[:, 1024:1024 + T].bitcast(I32)
        SY.quiet(lambda e: e.dma_start(posi, pos.to_broadcast([128, T])).then_inc(s_ld[2], 16))
        L_cst, L_pos, L_vec = (s_ld[0], 16), (s_ld[2], 16), (s_ld[3], 16)

        def pairs(us):
            for i in range(0, len(us), 2):
                groups.append(us[i:i + 2])
            return us

        U_f = pairs([unit(w_in[4 + i]) for i in range(4)])
        U_qq = pairs([unit(w_in[i]) for i in range(4)])
        U_lx = pairs([unit(w_in[16 + i]) for i in range(4)])
        U_lw = unit(lru_w)
        U_i = pairs([unit(w_iv[i]) for i in range(4)])
        U_lg = pairs([unit(w_in[20 + i]) for i in range(4)])
        U_g = pairs([unit(w_in[12 + i]) for i in range(4)])
        U_wo = pairs([unit(w_out[i]) for i in range(8)])
        def ada_kc(n):
            return n % 24 // 3, n // 24 * 3 + n % 3

        U_gate, U_up, U_ada, U_dn, ada_at = [], [], [], [], []
        for j in range(NF + 2):
            if j < NF:
                U_gate.append(unit(w_gu[j]))
                U_up.append(unit(w_gu[NF + j]))
                groups.append([U_gate[j], U_up[j]])
            n = len(U_ada)
            for _ in range(min(48 - n, 2 + (j < 5))):
                k, c = ada_kc(len(U_ada))
                U_ada.append(unit(ada[k * 128:(k + 1) * 128, c * 1024:(c + 1) * 1024]))
            ada_at.append(range(n, len(U_ada)))
            if j >= 2:
                U_dn.append(unit(w_down[j - 2]))
                if j < NF:
                    groups.append([U_dn[j - 2]])
        groups.append(U_dn[NF - 2:])
        U_sq = pairs([unit(w_in2[16 + i]) for i in range(4)])
        U_sk = pairs([unit(w_in2[20 + i]) for i in range(4)])
        U_sv = pairs([unit(w_sv[i]) for i in range(4)])
        U_rq = pairs([unit(w_in2[i]) for i in range(4)])
        U_rk = pairs([unit(w_in2[4 + i]) for i in range(4)])
        U_rv = pairs([unit(w_rv[i]) for i in range(4)])
        U_dec = [unit(decay[:, 0:1024]), unit(decay[:, 1024:2048])]
        U_rg = pairs([unit(w_in2[12 + i]) for i in range(4)])
        U_wo2 = pairs([unit(w_out2[i]) for i in range(8)])
        U_wq = pairs([unit(w_q[i], (cyc[0] + i % 8) % SLOTS) for i in range(16)])

        hk = lambda k: one_(hT, k)
        xk = lambda k: one_(xn, k)

        class Squares:

            def __init__(self, cols2=None):
                self.cols2, self.late, self.prev = cols2, None, {}

            def feed(self, k, t, free=()):
                s = 0 if k == 0 else 2 + (k - 1) % 6
                o = one_(sq, s)
                ta = act(o, hk(k), ACT.Square, t, *free, *self.prev.get(s, []))
                self.settle()
                self.late = (k, s, o, ta, free)

            def settle(self):
                if self.late is None:
                    return
                k, s, o, ta, free = self.late
                a1, a2 = one_(sq, 0), one_(sq, 1)
                self.late = None
                if k == KD - 1:
                    self.end = [ta]
                    if self.cols2 is not None:
                        self.end.append(ts(one_(sq, s + 1), o, self.cols2(k), MUL, ta, *self.prev[s + 1]))
                    return
                self.t = ta if k == 0 else tt(a1, a1, o, ADD, ta, self.t)
                if self.cols2 is not None:
                    if k == 0:
                        self.t = self.t2 = ts(a2, o, self.cols2(k), MUL, ta, *free)
                    else:
                        self.t2 = stt(a2, o, self.cols2(k), a2, MUL, ADD, ta, self.t2)
                self.prev[s] = [self.t] + ([self.t2] if self.cols2 is not None else [])

            def total(self, keep=(0, 0)):
                self.settle()
                if keep[0]:
                    keep_clock(keep[0])
                self.b = bank()
                n = T if self.cols2 is None else 2 * T
                t = [self.t] if self.cols2 is None else [self.t, self.t2]
                mm(pb[self.b][:, 0:n], c_("ones"), sq[:, 0:n], True, False, *t)
                self.t = mm(pb[self.b][:, 0:n], c_("ones"), sq[:, 2 * T:2 * T + n], False, True, *self.end, sig=True)
                if keep[1]:
                    keep_clock(keep[1])

            def rstd(self, keep, free=()):
                self.total(keep)
                return self.root(free)

            def root(self, free=()):
                t = act(stdt[:, 0:T], pb[self.b][:, 0:T], ACT.Ln, self.t, *free, scale=1.0 / D, bias=c_("eps"))
                readers[self.b] = [t]
                return t

        def inv_root(o, i, *t):
            return act(o, i, ACT.Exp, *t, scale=-0.5)

        def normed(squares, scale, shift, dst, t, t_free, h=X, full=False):

            def low(k, th):
                if shift is None:
                    return V.do(lambda e: e.tensor_tensor(h.lo(k), dst(k), h.hi(k).bitcast(F32), SUB), th, *t_free)
                return stt(h.lo(k), dst(k), shift(k), h.hi(k).bitcast(F32), ADD, SUB, th, *t_free)

            for k in range(KD):
                tk = stt(dst(k), hk(k), scale(k), t[0], MUL, MUL, t[1], *t_free)
                if shift is None:
                    h.th[k] = act(h.hi(k), dst(k), ACT.Copy, tk, *t_free)
                else:
                    h.th[k] = act(h.hi(k), dst(k), ACT.Identity, tk, *t_free, bias=shift(k))
                if k:
                    h.tl[k - 1] = low(k - 1, h.th[k - 1])
            h.tl[KD - 1] = low(KD - 1, h.th[KD - 1])
            return [ts(dst(k), dst(k), shift(k), ADD, h.th[k], h.tl[k]) for k in range(KD)] if full else []

        table(LNEXP)
        s0 = Squares()
        for k in range(KD):
            s0.feed(k, (s_x[k // 2], 16))
        for q in (P, V, A):
            q.wait(L_cst, L_vec)
        s0.total((0, 14))
        ahead(0, 1)
        t = s0.root()
        t_r0 = inv_root(one_(rstd, 0), one_(stdt, 0), t)
        act(one_r[:, :], c_("ones")[:, 0:128], ACT.Copy)
        t_pos = vcopy(cosT[:, :], posi, L_pos)
        normed(s0, lambda k: vc("mix", k), None, xk, (one_(rstd, 0), t_r0), (t_pos,))
        ahead(1, 2)
        fin2 = small[:, 128:136]
        t_fin2 = tt(fin2, vc("fin", 0, 8), vc("fin", 0, 8), MUL)

        lbm, e0, e1, lbd, oml = (small[:, 4 * i:4 * i + 4] for i in range(5))
        sp, su, sp_acc, nsp = (small[:, 20 + 8 * i:24 + 8 * i] for i in range(4))
        cs8 = small[:, 52:60]
        w2_ = small[:, 60:64]
        t = tt(lbm, vc("lb0", 0, 4), vc("lb1", 0, 4), MAX)
        ta = tt(e0, vc("lb0", 0, 4), lbm, SUB, t)
        tb = tt(e1, vc("lb1", 0, 4), lbm, SUB, t)
        t_ = ts(sp, vc("la", 0, 4), -1.0, MUL)
        t_ = tt(su, vc("la", 0, 4), sp, MAX, t_)
        ta = act(e0, e0, ACT.Exp, ta)
        tb = act(e1, e1, ACT.Exp, tb)
        te = act(su, su, ACT.Exp, t_, scale=-1.0)
        t = tt(e1, e0, e1, ADD, ta, tb)
        t = recip(e1, e1, t)
        t = tt(lbd, e0, e1, MUL, t)
        t_lb = ts(oml, lbd, -1.0, MUL, t, s2=1.0, op1=ADD)

        def softplus_table():
            t = ts(sp_acc, su, 2.0, ADD, te)
            t = recip(sp_acc, sp_acc, t)
            t = tt(su, su, sp_acc, MUL, t)
            t = tt(w2_, su, su, MUL, t)
            t = ts(sp_acc, w2_, 1.0 / 17, MUL, t, s2=1.0 / 15, op1=ADD)
            for n in (13, 11, 9, 7, 5, 3, 1):
                t = tt(sp_acc, sp_acc, w2_, MUL, t)
                t = ts(sp_acc, sp_acc, 1.0 / n, ADD, t)
            t = tt(sp_acc, sp_acc, su, MUL, t)
            t = ts(sp, sp, 0.0, MAX, t)
            t = stt(sp, sp_acc, 2.0, sp, MUL, ADD, t)
            return ts(nsp, sp, -LRU_C, MUL, t)

        def rope_tables():
            ang, kk_, rr_ = cosT[:, :], one_(stdt, 0), one_(stdt, 1)
            MAGIC = 12582912.0
            t = ts(ang, ang, c_("invf"), MUL, t_pos, t_r0)
            t = ts(kk_, ang, 1.0 / (2 * math.pi), MUL, t, s2=MAGIC, op1=ADD)
            t = ts(kk_, kk_, -MAGIC, ADD, t)
            c1 = 6.28125
            c2 = float(np.float32(round((2 * math.pi - c1) * 2 ** 21) / 2 ** 21))
            c3 = 2 * math.pi - c1 - c2
            for cc in (c1, c2, c3):
                t = stt(ang, kk_, -cc, ang, MUL, ADD, t)
            PI_ = 3.1415925
            t = ts(ang, ang, PI_, MIN, t, s2=-PI_, op1=MAX)
            t1 = act(sinT[:, :], ang, ACT.Sin, t)
            t2 = act(rr_, ang, ACT.Sin, t, scale=0.5)
            t = tt(rr_, rr_, rr_, MUL, t2)
            return [t1, ts(cosT[:, :], rr_, -2.0, MUL, t, t1, s2=1.0, op1=ADD)]

        sf, ff, kk, lf, bb, eb, kdec, qs, qdec, vtok, kstT, scT = (blk(i) for i in range(12))
        Sst = arena[:, 12 * 1024:14 * 1024]
        lx, xc, lg, gs = xn[:, 0:1024], xn[:, 1024:2048], bb, qs
        t_X = [*X.th.values(), *X.tl.values()]

        table(SIGM)
        t_z = V.do(lambda e: e.memset(scT, 0.0))
        t_sf, t_f = [], []
        for i in range(2):
            b, tk = gemm(U_f[2 * i:2 * i + 2], i == 0)
            t = act(half(sf, i), pb[b][:, :], ACT.Sigmoid, tk)
            readers[b] = [t]
            t_sf.append(t)
            for h in (2 * i, 2 * i + 1):
                t_f.append(ts(one_(ff, h), one_(sf, h), oml[:, h:h + 1], MUL, t, t_lb, s2=lbd[:, h:h + 1], op1=ADD))
        t_sp = softplus_table()
        t_k = ts(kk, ff, -1.0, MUL, *t_f, s2=1.0, op1=ADD)
        t_qs = []
        for i in range(2):
            b, tk = gemm(U_qq[2 * i:2 * i + 2])
            t = act(half(qs, i), pb[b][:, :], ACT.Sigmoid, tk)
            t = tt(half(qs, i), pb[b][:, :], half(qs, i), MUL, t)
            readers[b] = [t]
            t_qs.append(t)
            if i == 0:
                t_cs = act(cs8, vc("c", 0, 8), ACT.Sigmoid)
                t_c = tt(cs8, cs8, vc("c", 0, 8), MUL, t_cs)
        table(LNEXP)
        t_lf = act(lf, ff, ACT.Ln, *t_f)
        t = V.do(lambda e: e.memset(sq[:, 0:1024], 1.0), s0.t)
        t = V.do(lambda e: e.memset(sq[:, 0:1024:CH], 0.0), t)
        t_b = V.do(lambda e: e.tensor_tensor_scan(bb, sq[:, 0:1024], lf, 0.0, MUL, ADD), t, t_lf)
        bl = v3(bb, CH)[:, :, CH - 1:CH].broadcast_to([128, 32, CH])
        t_d = tt(v3(sf, CH), bl, v3(bb, CH), SUB, t_b, *t_f)
        t_eb = act(eb, bb, ACT.Exp, t_b)
        t_enb = act(kdec, bb, ACT.Exp, t_b, scale=-1.0)
        t_ed = act(sf, sf, ACT.Exp, t_d)
        t_kd = tt(kdec, kk, kdec, MUL, t_enb, t_k)
        t_ks = tt(sf, kk, sf, MUL, t_ed, t_k)
        t_qd = tt(qdec, qs, eb, MUL, t_eb, *t_qs)
        t_xc = []
        for i in range(2):
            b, tk = gemm(U_lx[2 * i:2 * i + 2])
            t = act(half(lx, i), pb[b][:, :], ACT.Copy, tk, *t_X)
            readers[b] = [t]
            for j in (2 * i, 2 * i + 1):
                tj = ts(one_(xc, j), one_(lx, j), vc("conv", 12 + j), MUL, t, *t_X, s2=vc("convb", j), op1=ADD)
                for tap in (2, 1, 0):
                    s = 3 - tap
                    tj = stt(xc[:, j * T + s:(j + 1) * T], lx[:, j * T:(j + 1) * T - s], vc("conv", tap * 4 + j),
                             xc[:, j * T + s:(j + 1) * T], MUL, ADD, tj)
                t_xc.append(tj)
        t_kT = []
        for tile in range(2):
            b = bank(4 + tile)
            for h in range(4):
                fn = lambda e, o=pb[b][:, h * 128:(h + 1) * 128], i=sf[:, h * T + tile * 128:h * T + tile * 128 + 128]: \
                    e.transpose(o, i, c_("ident"))
                tk = P.do(fn, t_ks)
            t = act(half(kstT, tile), pb[b][:, :], ACT.Copy, tk)
            readers[b] = [t]
            t_kT.append(t)
        t_sc = []
        hgm = c_("hgm").bitcast(U32).unsqueeze(1).broadcast_to([128, 4, 128])
        for tile in range(2):
            b = bank(6 + tile)
            for h in range(4):
                s = slice(h * T + tile * 128, h * T + tile * 128 + 128)
                tk = mm(pb[b][:, h * 128:(h + 1) * 128], kdec[:, s], qdec[:, s], True, True, t_kd, t_qd, sig=True)
            t = V.do(lambda e, o=v3(half(scT, tile), 128), i=v3(pb[b][:, :], 128): e.copy_predicated(o, hgm, i), tk, t_z)
            readers[b] = [t]
            t_sc.append(t)
        t_v = []
        bs, tk = gemm_tok(U_i)
        for tile in range(2):
            t = act(half(vtok, tile), pb[bs[tile]][:, :], ACT.Copy, tk)
            readers[bs[tile]] = [t]
            t_v.append(t)
        for hp in range(2):
            b = bank(6 + hp)
            for hh in range(2):
                h = 2 * hp + hh
                for tile in range(2):
                    mm(pb[b][:, hh * T + tile * 128:hh * T + tile * 128 + 128],
                       vtok[:, tile * 512 + h * 128:tile * 512 + h * 128 + 128],
                       scT[:, tile * 512 + h * 128:tile * 512 + h * 128 + 128], hh == 0 and tile == 0, False,
                       t_sc[tile], t_v[tile], skip=True)
        t_S, t_in = [None] * NCH, [None] * NCH
        NS = 4

        def Sof(c):
            return Sst[:, (c % NS) * 512:(c % NS + 1) * 512]

        def state_step(c):
            b = bank(4 + c % 2)
            tile, r = c // 4, 32 * (c % 4)
            for h in range(4):
                tk = mm(pb[b][:, h * 128:(h + 1) * 128], kstT[r:r + 32, tile * 512 + h * 128:tile * 512 + h * 128 + 128],
                        vtok[r:r + 32, tile * 512 + h * 128:tile * 512 + h * 128 + 128], True, True,
                        t_kT[tile], t_v[tile], sig=h == 3)
            fr = [t_in[c + 1 - NS]] if c + 1 - NS >= 1 else []
            if c == 0:
                t = vcopy(Sof(1), pb[b][:, :], tk)
            else:
                for h in range(4):
                    hs = slice(h * 128, (h + 1) * 128)
                    t = stt(Sof(c + 1)[:, hs], Sof(c)[:, hs], eb[:, h * T + c * CH + CH - 1:h * T + c * CH + CH],
                            pb[b][:, hs], MUL, ADD, tk, t_S[c], t_eb, *fr)
            readers[b] = [t]
            t_S[c + 1] = t

        def inter_step(c):
            if c == 0:
                return
            for h in range(4):
                tk = mm(pb[6 + h // 2][:, (h % 2) * T + c * CH:(h % 2) * T + (c + 1) * CH],
                        Sof(c)[:, h * 128:(h + 1) * 128], qdec[:, h * T + c * CH:h * T + (c + 1) * CH],
                        False, c == NCH - 1, t_S[c], sig=h == 3, skip=True)
            t_in[c] = tk

        def lru_gates():
            t_r, t_ig = [], []
            for gi, (dst, bias, lst) in enumerate(((ff, "ba", t_r), (lf, "bx", t_ig))):
                for i in range(2):
                    b = bank()
                    for jj in range(2):
                        j = 2 * i + jj
                        tk = mm(one_(pb[b], jj), slot(U_lw)[:, (gi * 4 + j) * 128:(gi * 4 + j + 1) * 128],
                                one_(xc, j), True, True, landed(U_lw), t_xc[j], sig=True)
                    for jj in range(2):
                        j = 2 * i + jj
                        t = act(one_(dst, j), one_(pb[b], jj), ACT.Sigmoid, tk, t_k, t_lf, t_b, bias=vc(bias, j))
                        lst.append(t)
                    readers[b] = [t]
            freed[U_lw] = [tk]
            return t_r, t_ig

        table(SIGM)
        t_r, t_ig = lru_gates()
        state_step(0)
        la_, th_, a_, ig_ = kk, lx, ff, lf
        t_la = [ts(one_(la_, j), one_(ff, j), nsp[:, j:j + 1], MUL, t_r[j], t_sp, t_kd, t_ks) for j in range(4)]
        t_th = act(th_, la_, ACT.Tanh, *t_la, *t_xc, scale=-1.0)
        t_i = tt(ig_, ig_, xc, MUL, *t_ig)
        t_lg, t_gs = [], []
        gx = sq[:, 1024:2048]
        for i in range(2):
            b, tk = gemm(U_lg[2 * i:2 * i + 2], mid=lambda i=i: (inter_step(2 * i), state_step(2 * i + 1)))
            t = act(half(lg, i), pb[b][:, :], ACT.Copy, tk, t_enb, t_eb, t_d)
            readers[b] = [t]
            g_, x_ = half(gx, i), half(lg, i)
            t = tt(g_, x_, x_, MUL, t)
            t = ts(g_, g_, 0.044715, MUL, t, s2=1.0, op1=ADD)
            t = tt(g_, g_, x_, MUL, t)
            t = act(g_, g_, ACT.Tanh, t, scale=math.sqrt(2.0 / math.pi))
            t = stt(g_, g_, 1.0, x_, ADD, MUL, t)
            t_lg.append(ts(g_, g_, 0.5, MUL, t))
            inter_step(2 * i + 1)
            state_step(2 * i + 2)
        table(LNEXP)
        t_a = act(a_, la_, ACT.Exp, *t_la)
        t = tt(la_, a_, a_, MUL, t_a, t_th)
        t = stt(la_, la_, 1.0, th_, ADD, MUL, t)
        t = act(la_, la_, ACT.Sqrt, t)
        t_bi = tt(la_, la_, ig_, MUL, t, t_i)
        t = V.do(lambda e: e.memset(a_[:, 0:1024:T], 0.0), t_bi)
        t_h = V.do(lambda e: e.tensor_tensor_scan(th_, a_, la_, 0.0, MUL, ADD), t)
        t_y = tt(th_, th_, gx, MUL, t_h, *t_lg)
        table(SIGM)
        for i in range(2):
            b, tk = gemm(U_g[2 * i:2 * i + 2], mid=lambda i=i: (inter_step(2 * i + 4), state_step(2 * i + 5) if i == 0 else None))
            t = act(half(gs, i), pb[b][:, :], ACT.Sigmoid, tk, t_qd)
            t = tt(half(gs, i), pb[b][:, :], half(gs, i), MUL, t)
            readers[b] = [t]
            t_gs.append(t)
            if i == 0:
                inter_step(5)
                state_step(6)
        t_win = tk
        inter_step(7)
        M = Halves(X.hi, X.lo)
        for k in range(4, 8):
            split_x(k, one_(th_, k - 4), t_y, M, free=(t_win,))
        table(LNEXP)
        tq, tm = [], []
        for hp in range(2):
            tq.append(act(half(sq, hp), pb[6 + hp][:, :], ACT.Square, t_in[NCH - 1], t_b))

        def hg_norm():
            for hp in range(2):
                b = bank(4 + hp)
                tk = mm(pb[b][:, :], c_("ones"), half(sq, hp), True, True, tq[hp], sig=True)
                t = act(half(stdt, 0), pb[b][:, :], ACT.Ln, tk, *tm[-1:], scale=1.0 / 128, bias=c_("eps"))
                readers[b] = [t]
                t = inv_root(half(rstd, 0), half(stdt, 0), t, *tm[-1:])
                t = stt(half(eb, hp), pb[6 + hp][:, :], vc("hgn"), half(rstd, 0), MUL, MUL, t, t_in[NCH - 1], tq[hp], *t_S[1:])
                readers[6 + hp] = [t]
                tm.append(t)
                t = tt(half(eb, hp), half(eb, hp), half(gs, hp), MUL, t, t_gs[hp])
                for k in (2 * hp, 2 * hp + 1):
                    split_x(k, one_(eb, k), t, M, free=(t_win,))

        def residual(us, h, first, squares, between, gate=None, free=()):
            rest = [k for k in range(KD) if k not in first]
            us = [us[2 * i:2 * i + 2] for i in range(4)]
            bs = []
            for i in range(3):
                take(us[i])
                bs.append(bank())
                for j, u in enumerate(us[i]):
                    products(one_(pb[bs[i]], j), u, kc, first, h, same, j == 0, False, False, skip=True)
                if i == 0:
                    between()
            for i in range(4):
                if i == 3:
                    take(us[3])
                    bs.append(bank())
                    for j, u in enumerate(us[3]):
                        products(one_(pb[bs[3]], j), u, kc, first, h, same, j == 0, False, False, skip=True)
                for j, u in enumerate(us[i]):
                    tk = products(one_(pb[bs[i]], j), u, kc, rest, h, same, False, True, True, skip=True)
                    used(u, tk)
                for j in range(2):
                    k = 2 * i + j
                    if gate is None:
                        tv = tt(hk(k), hk(k), one_(pb[bs[i]], j), ADD, tk)
                    else:
                        tv = stt(hk(k), one_(pb[bs[i]], j), gate(k), hk(k), MUL, ADD, tk)
                    squares.feed(k, tv, free)
                readers[bs[i]] = [tv]
                if i < 2:
                    ahead()
            return tk

        X.th, X.tl = {}, {}
        s1 = Squares()
        tp = residual(U_wo, M, [4, 5, 6, 7], s1, hg_norm, free=tm)
        t = s1.rstd((12, 10))
        t = inv_root(one_(rstd, 0), one_(stdt, 0), t)
        normed(s1, lambda k: vc("ffn", k), None, xk, (one_(rstd, 0), t), (tp, t_y), h=X)

        accm, acch, accl = arena[:, 2 * 1024:8 * 1024], more_lo[:, 6 * 1024:], more_lo[:, 0:6 * 1024]
        sgm = [arena[:, i * T:(i + 1) * T] for i in range(4)]
        atk = Halves(lambda j: one_(ahi, j), lambda j: one_(alo, j))
        table(SIGM)
        t_rope = rope_tables()
        table(SIGM)
        ringset[0] = [0, 1, 2]
        for b in range(4, 8):
            bank(b)
        t_dn = [None] * NF

        def ada_part(n):
            k, c = ada_kc(n)
            o, u = accm[:, c * 1024:(c + 1) * 1024], U_ada[n]
            if k == 0:
                t = ts(o, slot(u), cs8[:, 0:1], MUL, landed(u), t_c, *tm)
            else:
                t = stt(o, slot(u), cs8[:, k:k + 1], o, MUL, ADD, landed(u), t_ac[c])
            freed[u] = [t]
            t_ac[c] = t
            if k == KD - 1:
                ada_late.append(c)

        def ada_split(q=V, end=3):
            if ada_late and ada_late[0] < end:
                c = ada_late.pop(0)
                o, hi, lo = (a[:, c * 1024:(c + 1) * 1024] for a in (accm, acch, accl))
                t = act(hi, o, ACT.Copy, t_ac[c])
                t_ac[c] = q.do(lambda e: e.tensor_tensor(lo, o, hi.bitcast(F32), SUB), t, t_ac[c])

        ada_late = []

        t_ac = {}
        s2 = Squares(lambda k: fin2[:, k:k + 1])
        for j in range(NF + 2):
            if j < NF:
                b, tk = gemm([U_gate[j], U_up[j]], j == 0)
                s = sgm[j % 4]
                fr = [atk.th[j - 4], atk.tl[j - 4]] if j >= 4 else []
                t = act(s, one_(pb[b], 0), ACT.Sigmoid, tk, *fr, *t_ac.values() if j < 4 else ())
                t = tt(s, one_(pb[b], 0), s, MUL, t)
                t = tt(s, s, one_(pb[b], 1), MUL, t)
                readers[b] = [t]
                split_x(j, s, t, atk, slot_k=j % 4, free=[t_dn[j - 4]] if j >= 4 else [])
            ada_split(V if ada_late and ada_late[0] < 4 else G, 6)
            for n in ada_at[j]:
                ada_part(n)
            if 2 <= j < NF:
                k = j - 2
                take([U_dn[k]])
                for n in range(8):
                    tk = products(one_(pb[4 + n // 2], n % 2), U_dn[k], lambda _, n=n: kc(n), [k], atk, lambda k: k % 4,
                                  k == 0 and n % 2 == 0, False, n == 7, skip=True)
                used(U_dn[k], tk)
                t_dn[k] = tk
        while ada_late:
            ada_split(G, 6)
        mod = small[:, 64:112]

        def ada_sums(c0, c1):
            b = bank()
            for n in range(c0, c1):
                for part in (acch, accl):
                    tk = mm(pb[b][:, 2 * n:2 * n + 128], part[:, n * 128:(n + 1) * 128], one_r[:, :], part is acch, part is accl,
                            *(t_ac[n // 8] for n in range(c0, c1)), sig=n == c1 - 1 and part is accl)

            def take_sums():
                both = pb[b][:, 0:96].rearrange("p (n c) -> p n c", c=2)[:, :, 0]
                readers[b] = [tt(mod[:, c0:c1], both[:, c0:c1], vc("adab", c0, c1 - c0), ADD, tk)]
                return readers[b][0]
            return take_sums

        take(U_dn[NF - 2:], False)
        for i in range(4):
            for n in (2 * i, 2 * i + 1):
                for k in (NF - 2, NF - 1):
                    tk = products(one_(pb[4 + i], n % 2), U_dn[k], lambda _, n=n: kc(n), [k], atk, lambda k: k % 4,
                                  False, k == NF - 1, True, skip=True)
            for n in (2 * i, 2 * i + 1):
                tv = tt(hk(n), hk(n), one_(pb[4 + i], n % 2), ADD, tk)
                s2.feed(n, tv, (t_fin2,))
            readers[4 + i] = [tv]
        for u in U_dn[NF - 2:]:
            used(u, tk)
        table(LNEXP)
        ringset[0] = [0, 1, 2, 3]
        t_gu = tk
        sub = [subk_sb[:, 0:1024], subk_sb[:, 1024:2048]]
        for i in range(2):
            A.quiet(lambda e, i=i: e.dma_start(sub[i], subk[:, i * 1024:(i + 1) * 1024]).then_inc(s_ld[4], 16), tk)
        L_sub = s_ld[4], 32
        r1, r2 = one_(rstd, 0), one_(rstd, 1)
        t_mod = ada_sums(0, 24)()
        g1s, g2s = small[:, 112:120], small[:, 120:128]
        t1 = stt(g1s, mod[:, 8:16], 1.0, vc("n1", 0, 8), ADD, MUL, t_mod)
        t1 = tt(g1s, g1s, vc("fin", 0, 8), MUL, t1)
        t_mods = [t1, t_mod]
        s2.total()
        ahead(pool=True)
        s12 = pb[s2.b]
        t1 = vcopy(one_(stdt, 0), s12[:, 0:T], s2.t)
        t = stt(one_(stdt, 1), one_(stdt, 0), EPS, s12[:, T:2 * T], MUL, ADD, t1)
        readers[s2.b] = [t]
        t = act(one_(stdt, 1), one_(stdt, 1), ACT.Ln, t, scale=1.0 / D, bias=c_("eps2"))
        t_rr = inv_root(r2, one_(stdt, 1), t)
        t1 = act(one_(stdt, 0), one_(stdt, 0), ACT.Ln, t1, t, scale=1.0 / D, bias=c_("eps"))
        t_r1 = inv_root(r1, one_(stdt, 0), t1)
        late_sums = ada_sums(24, 48)
        normed(s2, lambda k: g1s[:, k:k + 1], lambda k: mod[:, k:k + 1], xk, (r2, t_rr), (*t_mods, t_gu, s2.t))
        t_X = [*X.th.values(), *X.tl.values()]
        t_x1 = [stt(hk(k), hk(k), vc("fin", k), r1, MUL, MUL, t_r1, *t_X) for k in range(KD)]
        t_mod2 = late_sums()
        t_g2s = stt(g2s, mod[:, 32:40], 1.0, vc("n2", 0, 8), ADD, MUL, t_mod2)

        rq2, rk2, sbq, sbk, rv, sv, rgs = (blk(i) for i in range(7))
        scR = [arena[:, 7 * 1024 + i * 384:7 * 1024 + (i + 1) * 384] for i in range(4)]
        w9 = 9 * 1024 - 512
        az, be, st = ([arena[:, w9 + (3 * a + i) * 384:w9 + (3 * a + i + 1) * 384] for i in range(3)] for a in range(3))
        raw, tmp, yr, ys = sq[:, 0:1024], sq[:, 1024:2048], xn[:, 0:1024], xn[:, 1024:2048]
        cb = cosT[:, :].unsqueeze(1).broadcast_to([128, 2, T])
        sb_ = sinT[:, :].unsqueeze(1).broadcast_to([128, 2, T])
        t_tmp = {0: s2.t, 1: s2.t}
        t_raw = {0: s2.t, 1: s2.t}

        def rope(us, dst):
            done = []

            def turn(i, t):
                b2 = bank()
                tk = mm(pb[b2][:, :], c_("rot"), half(raw, i), True, True, t, sig=True)
                ta = tt(v3(half(dst, i), T), v3(half(raw, i), T), cb, MUL, t, *t_rope, *t_ac.values())
                t = tt(v3(half(raw, i), T), v3(pb[b2][:, :], T), sb_, MUL, tk, ta)
                readers[b2] = [t]
                t_raw[i] = tt(half(dst, i), half(dst, i), half(raw, i), ADD, t)
                done.append(t_raw[i])

            for i in range(2):
                b, tk = gemm(us[2 * i:2 * i + 2])
                t = act(half(raw, i), pb[b][:, :], ACT.Copy, tk, t_raw[i])
                readers[b] = [t]
                hooks()
                steps.insert(0, lambda i=i, t=t: turn(i, t))
            return done

        def group_rms(src, gain, i, dst, *t):
            tq = act(half(tmp, i), src, ACT.Square, t_tmp[i], *t)
            b = bank()
            tk = mm(pb[b][:, :], c_("bd64"), half(tmp, i), True, True, tq, sig=True)
            ta = act(half(tmp, i), pb[b][:, :], ACT.Ln, tk, bias=c_("eps"))
            readers[b] = [ta]
            tr = inv_root(half(tmp, i), half(tmp, i), ta)
            t_tmp[i] = stt(dst, src, gain, half(tmp, i), MUL, MUL, tr)
            return t_tmp[i]

        def head_scores(kT, qT, h, t):
            r, j = 64 * (h % 2), h // 2
            b = bank()
            mm(pb[b][:, 0:T], kT[r:r + 64, j * T:j * T + 128], qT[r:r + 64, j * T:(j + 1) * T], True, True, *t)
            tk = mm(pb[b][:, T:T + 128], kT[r:r + 64, j * T + 128:(j + 1) * T], qT[r:r + 64, j * T + 128:(j + 1) * T],
                    True, True, sig=True)
            return b, tk

        def head_out(w, v, h, b, t):
            r, o = 64 * (h % 2), (h // 2 % 2) * T
            mm(pb[b][r:r + 64, o:o + T], v[:, h * 64:(h + 1) * 64], w[:, 0:T], True, False, *t, skip=True)
            return mm(pb[b][r:r + 64, o + 128:o + T], v[:, 512 + h * 64:512 + (h + 1) * 64], w[:, T:T + 128],
                      False, True, sig=True, skip=True)

        def normed_heads(us, dst, gain):
            done = []
            for i in range(2):
                b, tk = gemm(us[2 * i:2 * i + 2], us is U_sq and i == 0)
                t = act(half(dst, i), pb[b][:, :], ACT.Copy, tk, *t_ac.values())
                readers[b] = [t]
                steps.append(lambda i=i, t=t: done.append(group_rms(half(dst, i), gain, i, half(dst, i), t)))
            return done

        def token_major(us, dst):
            done = []
            bs, tk = gemm_tok(us)
            for tile in range(2):
                t = act(half(dst, tile), pb[bs[tile]][:, :], ACT.Copy, tk, *t_ac.values())
                readers[bs[tile]] = [t]
                done.append(t)
            return done

        t_sq = normed_heads(U_sq, sbq, vc("sbq"))
        t_sk = normed_heads(U_sk, sbk, vc("sbk"))
        t_sv = token_major(U_sv, sv)

        sbm = c_("sbm").unsqueeze(1).broadcast_to([128, 2, 128])

        def diag(ap):
            return bass.AP(ap.tensor, ap.offset, [ap.ap[0], [256, 2], [1, 128]])

        t_be, t_st, t_w, t_ys, t_cum = {}, {}, {}, {}, {}

        def sb_logits(h):
            n = h % 3
            b, tk = head_scores(sbk, sbq, h, [*t_sq, *t_sk])
            t_abs = act(az[n], pb[b][:, 0:384], ACT.Abs, tk, *([t_ys[h - 3]] if h >= 3 else [s2.t]), scale=0.125)
            t = act(az[n], az[n], ACT.Exp, t_abs, scale=-1.0)
            t = act(az[n], az[n], ACT.Ln, t, bias=c_("one"))
            tb = ts(be[n], pb[b][:, 0:384], 0.125, MUL, t_abs, *([t_w[h - 3]] if h >= 3 else []), s2=0.0, op1=MIN)
            tb = tt(be[n], be[n], az[n], SUB, tb, t)
            t = stt(st[n], pb[b][:, 0:384], -0.125, be[n], MUL, ADD, tb, *([t_cum[h - 3]] if h >= 3 else []))
            readers[b] = [t]
            t_be[h] = tb
            t_st[h] = tt(diag(st[n]), diag(st[n]), sbm, MUL, t)

        def sb_weights(h):
            n = h % 3
            b = bank()
            mm(pb[b][:, 0:384], c_("tri"), st[n], True, False, t_st[h], skip=True)
            tk = mm(pb[b][:, 128:256], c_("ones"), st[n][:, 256:384], False, True, sig=True, skip=True)
            t_cum[h] = tk
            t = tt(be[n], be[n], pb[b][:, 0:384], ADD, tk, t_be[h])
            readers[b] = [t]
            t = act(az[n], be[n], ACT.Exp, t)
            t_w[h] = tt(diag(az[n]), diag(az[n]), sbm, MUL, t)

        def sb_out(h):
            if h % 4 == 0:
                bank(6 + h // 4)
            t_ys[h] = head_out(az[h % 3], sv, h, 6 + h // 4, [t_w[h], *t_sv])

        def sb_step(i):
            if i < 8:
                sb_logits(i)
            if 1 <= i <= 8:
                sb_weights(i - 1)
            if 2 <= i:
                sb_out(i - 2)

        M = Halves(X.hi, X.lo)
        t_sbn = {}

        def sb_norm(i):
            t = act(half(ys, i), pb[6 + i][:, :], ACT.Copy, t_ys[4 * i + 3], *t_X)
            readers[6 + i] = [t]
            t_sbn[i] = group_rms(half(ys, i), vc("sbo"), i, half(ys, i), t)

        steps += [lambda i=i: sb_step(i) for i in range(10)]
        steps += [lambda i=i: sb_norm(i) for i in range(2)]
        hooks()
        t_rq = rope(U_rq, rq2)
        hooks()
        t_rk = rope(U_rk, rk2)
        hooks(2)
        t_rv = token_major(U_rv, rv)
        hooks()

        t_scR, t_yr = {}, {}

        def ret_scores(h):
            b, tk = head_scores(rk2, rq2, h, [*t_rq, *t_rk])
            dec = slot(U_dec[h // 4])[:, (h % 4) * T:(h % 4 + 1) * T]
            w = scR[h % 4]
            fr = [t_yr[h - 4]] if h >= 4 else []
            tt(w[:, 0:T], pb[b][:, 0:T], dec, MUL, tk, landed(U_dec[h // 4]), *fr)
            t = tt(w[:, T:T + 128], pb[b][:, T:T + 128], dec[:, 0:128], MUL)
            readers[b] = [t]
            t_scR[h] = t
            freed[U_dec[h // 4]] = [t]

        def ret_out(h):
            if h % 4 == 0:
                bank(4 + h // 4)
            t_yr[h] = head_out(scR[h % 4], rv, h, 4 + h // 4, [t_scR[h], *t_rv])

        t_rg = []
        t_yc = {}

        def ret_mean(i):
            t = act(half(yr, i), pb[4 + i][:, :], ACT.Copy, t_yr[4 * i + 3], *t_X)
            readers[4 + i] = [t]
            b = bank()
            tk = mm(pb[b][:, :], c_("bd64"), half(yr, i), True, True, t, sig=True)
            t = tt(half(yr, i), half(yr, i), pb[b][:, :], SUB, tk)
            readers[b] = [t]
            t_yc[i] = t

        for h in range(4):
            ret_scores(h)
            if h:
                ret_out(h - 1)
            if h == 2:
                hooks()
        b, tk = gemm(U_rg[0:2])
        t_rg0 = act(half(rgs, 0), pb[b][:, :], ACT.Copy, tk, *t_ac.values())
        readers[b] = [t_rg0]
        for h in range(4, 8):
            ret_scores(h)
            ret_out(h - 1)
            if h == 5:
                ret_mean(0)
                hooks(12)
        ret_out(7)
        ret_mean(1)

        def ret_norms():
            tq = [act(half(tmp, i), half(yr, i), ACT.Square, t_yc[i], t_tmp[i]) for i in range(2)]
            bs = [bank(), bank()]
            tks = [mm(pb[bs[i]][:, :], c_("bd64"), half(tmp, i), True, True, tq[i], sig=True) for i in range(2)]
            for i in range(2):
                ta = act(half(tmp, i), pb[bs[i]][:, :], ACT.Ln, tks[i], bias=c_("eps"))
                readers[bs[i]] = [ta]
                t_tmp[i] = inv_root(half(tmp, i), half(tmp, i), ta)
                for k in (2 * i, 2 * i + 1):
                    t_yc[i] = stt(one_(yr, k), one_(yr, k), vc("retg", k), one_(tmp, k), MUL, MUL, t_tmp[i])
            table(SIGM)
            t = act(half(raw, 0), half(rgs, 0), ACT.Sigmoid, t_rg0, t_raw[0])
            t_rg.append(tt(half(rgs, 0), half(rgs, 0), half(raw, 0), MUL, t))

        b, tk = gemm(U_rg[2:4], mid=ret_norms)
        t_win2 = tk
        for i in range(2):
            for k in (2 * i, 2 * i + 1):
                split_x(4 + k, one_(ys, k), t_sbn[i], M, free=(t_win2,))
        t = act(half(raw, 1), pb[b][:, :], ACT.Sigmoid, tk, t_raw[1])
        t = tt(half(rgs, 1), pb[b][:, :], half(raw, 1), MUL, t, *t_ac.values())
        readers[b] = [t]
        t_rg.append(t)
        table(LNEXP)

        def gated():
            late = None
            for k in range(4):
                t = tt(one_(yr, k), one_(yr, k), one_(rgs, k), MUL, t_yc[k // 2], t_rg[k // 2])
                M.th[k] = act(M.hi(k), one_(yr, k), ACT.Copy, t, t_win2)
                if late is not None:
                    low(late, t)
                late = k
            low(late, t)

        def low(k, t):
            M.tl[k] = V.do(lambda e: e.tensor_tensor(M.lo(k), one_(yr, k), M.hi(k).bitcast(F32), SUB), M.th[k], t, t_win2)

        s3 = Squares()
        tp = residual(U_wo2, M, [4, 5, 6, 7], s3, gated, gate=lambda k: mod[:, 16 + k:17 + k],
                      free=(*t_x1, *t_tmp.values(), *t_rg))
        t = s3.rstd((8, 10))
        t = inv_root(one_(rstd, 0), one_(stdt, 0), t)
        X = Halves(X.hi, X.lo)
        t_h2 = normed(s3, lambda k: g2s[:, k:k + 1], lambda k: mod[:, 24 + k:25 + k], xk, (one_(rstd, 0), t),
                      (tp, *M.tl.values(), *M.th.values(), t_g2s), h=X, full=True)
        t_X = [*t_h2]

        SC = [blk(0, 2048), blk(2, 2048)]
        h2t, x2t, g2b = [blk(4), blk(5)], sq[:, 0:1024], subk_sb[:, 0:1024]
        pk = arena[:, 9 * 1024:12 * 1024]
        dgr = [arena[:, 12 * 1024 + i * 128:12 * 1024 + (i + 1) * 128] for i in range(16)]
        qry = [sq[:, 0:512], sq[:, 512:1024]]
        dg = sq[:, 1024:2048]
        f32c = lambda o, n: pk[:, o:o + n]
        tsv, tif, abf, iab = f32c(0, 32), f32c(32, 32), f32c(64, 32), f32c(96, 32)
        bsv, nb, ssum = f32c(128, 16), f32c(144, 1), f32c(145, 1)
        sc2 = f32c(160, 256)
        cand, cand2 = f32c(416, 256), f32c(672, 256)
        eq = f32c(928, 512)
        gts, aa, ae, ex = f32c(1440, 256), f32c(1696, 256), f32c(1952, 256), f32c(2208, 256)

        t_SC = {}
        t_sco = {}

        def query(h, mid):
            b, tk = gemm(U_wq[2 * h:2 * h + 2], h == 0, mid)
            t = act(qry[h % 2], pb[b][:, :], ACT.Copy, tk, s3.t, *([t_sco[h - 2]] if h >= 2 else []))
            readers[b] = [t]
            t_qry[h] = t

        t_qry = {}

        def scores(h):
            b = bank()
            for tile in range(2):
                for p in range(2):
                    c = (2 * h + p) % 8
                    tk = mm(pb[b][:, (2 * tile + p) * 128:(2 * tile + p + 1) * 128],
                            qry[h % 2][:, p * T + tile * 128:p * T + tile * 128 + 128], sub[h // 4][:, c * 128:(c + 1) * 128],
                            True, True, t_qry[h], L_sub, sig=True)
            t_sco[h] = tk
            for tile in range(2):
                t = act(SC[tile][:, h * 256:(h + 1) * 256], pb[b][:, tile * 256:(tile + 1) * 256], ACT.Copy, tk)
            readers[b] = [t]
            t_SC[h] = t

        def turned(src, dst, tile, t0, free=()):
            lst = []
            for g in range(2):
                b = bank()
                for n in range(4):
                    fn = lambda e, o=pb[b][:, n * 128:(n + 1) * 128], \
                        i=src(4 * g + n)[:, tile * 128:(tile + 1) * 128]: e.transpose(o, i, c_("ident"))
                    tk = P.do(fn, *t0)
                t = act(dst[:, g * 512:(g + 1) * 512], pb[b][:, :], ACT.Copy, tk, *free)
                readers[b] = [t]
                lst.append(t)
            return lst

        def gate_rows():
            lst = []
            for g in range(2):
                b = bank()
                for n in range(4):
                    k = 4 * g + n
                    t = ts(dg[:, k * 128:(k + 1) * 128], c_("ident"), mod[:, 40 + k:41 + k], MUL, s3.t)
                    tk = mm(pb[b][:, n * 128:(n + 1) * 128], c_("ones"), dg[:, k * 128:(k + 1) * 128], True, True, t,
                            sig=True)
                t = act(g2b[:, g * 512:(g + 1) * 512], pb[b][:, :], ACT.Copy, tk, t_sco[7])
                readers[b] = [t]
                lst.append(t)
            return lst

        def top16(src, tmp_, vals, idx, *t):
            t1 = V.do(lambda e: e.max(vals[:, 0:8], src), *t)
            V.do(lambda e: e.max_index(idx[:, 0:8], vals[:, 0:8], src), t1)
            t1 = V.do(lambda e: e.match_replace(tmp_, vals[:, 0:8], src, NEG), t1)
            t1 = V.do(lambda e: e.max(vals[:, 8:16], tmp_), t1)
            return V.do(lambda e: e.max_index(idx[:, 8:16], vals[:, 8:16], tmp_), t1)

        t_ids, t_gt = {}, {}

        def choose(n):
            tile, h = n // 8, n % 8
            for p in range(2):
                s = SC[tile][:, (2 * h + p) * 128:(2 * h + p + 1) * 128]
                t = top16(s, sc2[:, 0:128], tsv[:, p * 16:p * 16 + 16], tiu[:, p * 16:p * 16 + 16],
                          t_SC[h], (V.sem, V.n))
            tf = vcopy(tif, tiu[:, :], t)
            t = tt(v3(cand, 16), tsv[:, 0:16].unsqueeze(2).broadcast_to([128, 16, 16]),
                   tsv[:, 16:32].unsqueeze(1).broadcast_to([128, 16, 16]), ADD, t)
            exn = ex[:, n * 16:(n + 1) * 16]
            t = top16(cand, cand2, bsv, bcu[:, :], t, *([t_gt[n - 1][0]] if n else []))
            tn = ts(nb, bsv[:, 0:1], -1.0, MUL, t)
            te = act(exn, bsv, ACT.Exp, tn, bias=nb, accum_out=ssum)
            ta = V.do(lambda e: e.tensor_scalar(abu[:, 0:16], bcu[:, :], 4, None, ALU.logical_shift_right), t)
            tb = V.do(lambda e: e.tensor_scalar(abu[:, 16:32], bcu[:, :], 15, None, ALU.bitwise_and), t)
            t = vcopy(abf, abu[:, :], ta, tb)
            t = tt(v3(eq, 16), c_("iota").unsqueeze(1).broadcast_to([128, 32, 16]),
                   abf.unsqueeze(2).broadcast_to([128, 32, 16]), ALU.is_equal, t)
            e4 = eq.rearrange("p (a s m) -> p a s m", a=2, m=16)
            t = tt(e4, e4, tif.rearrange("p (a m) -> p a m", a=2).unsqueeze(2).broadcast_to([128, 2, 16, 16]), MUL, t, tf)
            t = V.do(lambda e: e.tensor_reduce(iab, v3(eq, 16), AX_X, ADD), t)
            t_ids[n] = stt(idsb[:, n * 16:(n + 1) * 16], iab[:, 0:16], 128.0, iab[:, 16:32], MUL, ADD, t)
            tr = recip(ssum, ssum, te)
            t = ts(gts[:, n * 16:(n + 1) * 16], exn, ssum, MUL, tr)
            t_gt[n] = (te, t)

        others = [p for p in range(SLOTS) if p not in {place[u] for u in U_wq}]
        rows_at = [ring_sb[:, p * 1024:(p + 1) * 1024] for p in range(SLOTS)]
        rows_at += [blk(6), blk(7), blk(8), xn[:, 0:1024], xn[:, 1024:2048]]
        fifo = [(p, freed[last[p]]) for p in others] + [(SLOTS + i, t_X) for i in range(3)]
        row_uses = [0] * len(rows_at)

        def gather(table_, col, tk_ids):
            s, free = fifo.pop(0)
            o = rows_at[s]
            row_uses[s] += 1
            G.quiet(lambda e: e.indirect_dma_start(
                o, None, table_, bass.IndirectOffsetOnAxis(ap=idsb[:, col:col + 1], axis=0)).then_inc(s_row[s], 16),
                tk_ids, *free)
            return s, o, (s_row[s], 16 * row_uses[s])

        R = 4
        NB = 256 // R
        BPC = 16 // R
        downs = {}
        t_mmu = {}

        def down_rows(i):
            downs[i] = [gather(peer_down, i * R + j, t_ids[i // BPC]) for j in range(R)]

        def down_dots(i):
            tile = i // (NB // 2)
            for j in range(R):
                s, o, tl = downs[i][j]
                col = i * R + j
                t = V.do(lambda e, o=o, col=col, tile=tile: e.tensor_tensor_reduce(
                    o, o, h2t[tile], 1.0, 0.0, MUL, ADD, aa[:, col:col + 1]), tl, *t_h2t[tile])
                fifo.append((s, [t]))
            return act(ae[:, i * R:i * R + R], aa[:, i * R:i * R + R], ACT.Gelu, t)

        def weights_of(i, te):
            cols = slice(i * R, i * R + R)
            t = tt(ae[:, cols], ae[:, cols], gts[:, cols], MUL, te, t_gt[i // BPC][1])
            return [act(dgr[col % 16], c_("ident"), ACT.Copy, t, *([t_mmu[col - 16]] if col >= 16 else []),
                        scale=ae[:, col:col + 1]) for col in range(i * R, i * R + R)]

        ups = {}

        def prepare(i):
            if i + 1 < NB and i + 1 not in downs:
                down_rows(i + 1)
            te = down_dots(i)
            if i % BPC == 1 and i // BPC + 2 < 16:
                choose(i // BPC + 2)
            t_dg = weights_of(i, te)
            ups[i] = [(*gather(peer_up, i * R + j, t_ids[i // BPC]), t_dg[j]) for j in range(R)]

        def add_rows(i):
            tile = i // (NB // 2)
            for j in range(R):
                s, o, tl, t_d = ups[i][j]
                col = i * R + j
                first, end = col % 128 == 0, col % 128 == 127
                if first:
                    bank(4 + 2 * tile)
                    bank(5 + 2 * tile)
                tk0 = mm(pb[4 + 2 * tile][:, :], dgr[col % 16], o[:, 0:512], first, end, tl, t_d, sig=end)
                tk = mm(pb[5 + 2 * tile][:, :], dgr[col % 16], o[:, 512:1024], first, end, sig=True)
                t_mmu[col] = tk
                fifo.append((s, [tk]))
            return tk0, tk

        def finish(tile, tks):
            for g in range(2):
                gsl = slice(g * 512, (g + 1) * 512)
                t = tt(dg[:, gsl], pb[4 + 2 * tile + g][:, :], g2b[:, gsl], MUL, tks[g], *t_g2, (V.sem, V.n))
                t = tt(x2t[:, gsl], x2t[:, gsl], dg[:, gsl], ADD, t, *t_x2t)
                A.quiet(lambda e, gsl=gsl: e.dma_start(out[tile * 128:(tile + 1) * 128, gsl], x2t[:, gsl]).then_inc(s_out, 16), t)

        def done_query(h):
            fifo.extend((place[u], freed[u]) for u in U_wq[2 * h:2 * h + 2] if last[place[u]] == u)

        query(0, None)
        done_query(0)
        scores(0)
        choose(0)
        t_h2t = [turned(xk, h2t[tile], tile, t_X) for tile in range(2)]
        fifo += [(SLOTS + 3 + i, [x for t in t_h2t for x in t]) for i in range(2)]
        down_rows(0)
        down_rows(1)
        for h in range(1, 8):
            query(h, (lambda: scores(h - 1)) if h > 1 else None)
            done_query(h)
            if h in (2, 3, 5, 6):
                prepare({2: 0, 3: 1, 5: 2, 6: 3}[h])
            if h == 2:
                choose(1)
            if h in (4, 5, 6):
                add_rows(h - 4)
        scores(7)
        t_g2 = gate_rows()
        for i in range(4, NB + 1):
            if i < NB:
                prepare(i)
            if i == NB - 1:
                keep_clock(10)
            tk = add_rows(i - 1)
            if i % (NB // 2) == NB // 2 - 4:
                t_x2t = turned(hk, x2t, i // (NB // 2), [s3.t], [t_sco[7]] if i < NB // 2 else [(s_out, 32)])
            if i % (NB // 2) == 0:
                finish(i // (NB // 2) - 1, tk)

        for u, src in enumerate(units):
            SY.quiet(lambda e, u=u, src=src: e.dma_start(slot(u), src).then_inc(s_slot[place[u]], 16),
                     *(freed[before[u]] if before[u] is not None else []))
        SY.wait((s_out, 64))

        block = ctx.enter_context(nc.Block())

        @block.sync
        def _(e):
            SY.run(e)

        @block.gpsimd
        def _(e):
            G.run(e)

        @block.scalar
        def _(e):
            A.run(e)

        @block.vector
        def _(e):
            V.run(e)

        @block.tensor
        def _(e):
            P.run(e)


def kernel(**inputs):
    import numpy as _np
    import concourse.bacc as _bacc
    from concourse import mybir as _mybir
    from concourse.bass_utils import run_bass_kernel_spmd as _run

    a = {k: _np.asarray(v) for k, v in inputs.items()}

    def fm(v):
        return v.reshape(-1, 128).T

    def units(w):
        n = w.shape[1] // 128
        return _np.ascontiguousarray(w.reshape(8, 128, n, 128).transpose(2, 1, 0, 3)).reshape(n, 128, 1024)

    def rows(w):
        return _np.ascontiguousarray(w.reshape(4, 2, 128, 512).transpose(0, 2, 1, 3)).reshape(4, 128, 1024)

    def twice(v):
        return _np.concatenate([v.reshape(-1), v.reshape(-1)]).reshape(128, 1)

    vecs = _np.concatenate([
        fm(a["mix_norm_w"]), fm(a["ffn_norm_w"]), fm(a["final_norm_w"]), fm(a["norm1_gain_2"]), fm(a["norm2_gain_2"]),
        fm(a["conv_w"][0]), fm(a["conv_b"]), fm(a["lru_ba"]), fm(a["lru_bx"]), fm(a["lru_a"]),
        fm(a["hg_lb"][0]), fm(a["hg_lb"][1]), fm(a["hg_norm_w"]), fm(a["ret_norm_gain_2"]),
        twice(a["sb_q_gain_2"]), twice(a["sb_k_gain_2"]), twice(a["sb_out_gain_2"]), fm(a["ada_b_2"]), fm(a["c_2"]),
    ], axis=1)
    lw = _np.zeros((128, 8, 128), _np.float32)
    for g, w in enumerate((a["lru_wa"][0], a["lru_wx"][0])):
        for j in range(4):
            lw[0:64, g * 4 + j, 0:64] = w[2 * j]
            lw[64:128, g * 4 + j, 64:128] = w[2 * j + 1]
    cst, dec = shape_constants()
    arrays = {
        "xT": a["x"][0].T.reshape(8, 128, 256).transpose(1, 0, 2).reshape(128, 2048),
        "vecs": vecs, "cst": cst, "decay": dec, "pos": a["positions_2"],
        "w_in": units(a["w_in"][0]), "w_out": units(a["w_out"][0]), "w_gu": units(a["w_gate_up"][0]),
        "w_down": a["w_down"][0].reshape(22, 128, 1024), "ada": a["ada_w_2"][0],
        "w_in2": units(a["w_in_2"][0]), "w_out2": units(a["w_out_2"][0]), "w_q": units(a["peer_w_query_2"][0]),
        "w_iv": rows(a["w_in"][0][:, 1024:1536]), "w_sv": rows(a["w_in_2"][0][:, 3072:3584]),
        "w_rv": rows(a["w_in_2"][0][:, 1024:1536]),
        "subk": a["peer_sub_keys_2"][0].reshape(16, 128, 128).transpose(2, 0, 1).reshape(128, 2048),
        "lru_w": lw.reshape(128, 1024),
        "peer_down": a["peer_down_2"][0], "peer_up": a["peer_up_2"][0],
    }
    nc = _bacc.Bacc("TRN2", target_bir_lowering=False, num_devices=1)
    feed, args = {}, []
    for name, v in arrays.items():
        v = _np.ascontiguousarray(v)
        feed[f"in_{name}"] = v
        args.append(nc.dram_tensor(f"in_{name}", v.shape, _mybir.dt.from_np(v.dtype), kind="ExternalInput").ap())
    o = nc.dram_tensor("out_0", (256, 1024), _mybir.dt.float32, kind="ExternalOutput").ap()
    build(nc, *args, o)
    r = _run(nc, [feed], core_ids=[0])
    return r.results[0]["out_0"].reshape(1, 256, 1024)
```
